# Optimizing a Trainium2 kernel written in Bass

```python
import jax, jax.numpy as jnp
from jax import lax
import numpy as np
import math

D_MODEL = 1024
BATCH = 1
SEQ = 256
DEPTH = 2

N_A = DEPTH // 2
N_B = DEPTH - N_A
M_HEADS = 4
M_DQK = 128
M_DV = D_MODEL // M_HEADS
M_CHUNK = 64
M_SPLITS = [M_HEADS * M_DQK, 2 * M_HEADS * M_DQK, 2 * M_HEADS * M_DQK + M_HEADS * M_DV,
            2 * M_HEADS * M_DQK + 2 * M_HEADS * M_DV, 2 * M_HEADS * M_DQK + 2 * M_HEADS * M_DV + M_HEADS]
M_IN = 2 * M_HEADS * M_DQK + 2 * M_HEADS * M_DV + 2 * M_HEADS
A_HEADS = 8
A_DH = D_MODEL // A_HEADS
ROT_DIM = A_DH // 4
ROPE_THETA = 500000.0
MOBA_BLOCK = 256
MOBA_TOPK = 3
Q_BLOCK = 128
D_FF = 2816
CONV_W = 3
EPS = 1e-6


def rmsnorm(x, g):
    xf = x.astype(jnp.float32)
    y = xf * lax.rsqrt(jnp.mean(xf * xf, axis=-1, keepdims=True) + EPS)
    return (y * g.astype(jnp.float32)).astype(x.dtype)

def rope_tables(s_len):
    pos = jnp.arange(s_len, dtype=jnp.float32)
    inv = ROPE_THETA ** (-jnp.arange(0, ROT_DIM, 2, dtype=jnp.float32) / ROT_DIM)
    ang = pos[:, None] * inv[None, :]
    return jnp.cos(ang), jnp.sin(ang)

def apply_partial_rope(t, cos, sin):
    half = ROT_DIM // 2
    t1, t2, rest = t[..., :half], t[..., half:ROT_DIM], t[..., ROT_DIM:]
    c = cos[None, :, None, :].astype(t.dtype)
    s = sin[None, :, None, :].astype(t.dtype)
    return jnp.concatenate([t1 * c - t2 * s, t2 * c + t1 * s, rest], axis=-1)

def mlstm_chunkwise(q, k, v, i_pre, f_pre):
    b_, s_, h_, dk = q.shape
    nc = s_ // M_CHUNK

    def to_chunks(t):
        t = t.astype(jnp.float32).reshape((b_, nc, M_CHUNK, h_) + t.shape[3:])
        return jnp.moveaxis(jnp.moveaxis(t, 1, 0), 3, 2)

    qc, kc, vc = to_chunks(q), to_chunks(k), to_chunks(v)
    ic = to_chunks(i_pre)
    lfc = to_chunks(jax.nn.log_sigmoid(f_pre.astype(jnp.float32)))
    tri = jnp.tril(jnp.ones((M_CHUNK, M_CHUNK), dtype=bool))

    def step(carry, inp):
        c_st, n_st, m_st = carry
        qb, kb, vb, ib, lfb = inp
        bcum = jnp.cumsum(lfb, axis=-1)
        dmat = jnp.where(tri, bcum[..., :, None] - bcum[..., None, :] + ib[..., None, :], -jnp.inf)
        inter = bcum + m_st[..., None]
        m_t = jnp.maximum(inter, jnp.max(dmat, axis=-1))
        w_inter = jnp.exp(inter - m_t)
        s = jnp.einsum('bhtd,bhsd->bhts', qb, kb) * jnp.exp(dmat - m_t[..., None])
        num = w_inter[..., None] * jnp.einsum('bhtd,bhde->bhte', qb, c_st) + jnp.einsum('bhts,bhse->bhte', s, vb)
        den = w_inter * jnp.einsum('bhtd,bhd->bht', qb, n_st) + jnp.sum(s, axis=-1)
        h = num / jnp.maximum(jnp.abs(den), jnp.exp(-m_t))[..., None]
        b_last = bcum[..., -1]
        g = b_last[..., None] - bcum + ib
        m_new = jnp.maximum(b_last + m_st, jnp.max(g, axis=-1))
        decay = jnp.exp(b_last + m_st - m_new)
        wk = jnp.exp(g - m_new[..., None])[..., None] * kb
        c_new = decay[..., None, None] * c_st + jnp.einsum('bhsd,bhse->bhde', wk, vb)
        n_new = decay[..., None] * n_st + jnp.sum(wk, axis=-2)
        return (c_new, n_new, m_new), h

    dv = v.shape[-1]
    init = (jnp.zeros((b_, h_, dk, dv), jnp.float32), jnp.zeros((b_, h_, dk), jnp.float32),
            jnp.zeros((b_, h_), jnp.float32))
    _, hs = lax.scan(step, init, (qc, kc, vc, ic, lfc))
    return jnp.transpose(hs, (1, 0, 3, 2, 4)).reshape(b_, s_, h_, dv)

def mlstm_mixer(x, norm_g, w_in, b_gates, h_norm_g, w_out):
    b_, s_, _ = x.shape
    u = rmsnorm(x, norm_g) @ w_in
    q, k, v, o, gi, gf = jnp.split(u, M_SPLITS, axis=-1)
    q = q.reshape(b_, s_, M_HEADS, M_DQK) * (M_DQK ** -0.5)
    k = k.reshape(b_, s_, M_HEADS, M_DQK)
    v = v.reshape(b_, s_, M_HEADS, M_DV)
    i_pre = gi.astype(jnp.float32) + b_gates[0]
    f_pre = gf.astype(jnp.float32) + b_gates[1]
    h = mlstm_chunkwise(q, k, v, i_pre, f_pre)
    h = rmsnorm(h, h_norm_g.reshape(M_HEADS, M_DV)).reshape(b_, s_, M_HEADS * M_DV)
    h = h * jax.nn.sigmoid(o.astype(jnp.float32))
    return h.astype(x.dtype) @ w_out

def conv_ffn(x, norm_g, w_up, conv_w, conv_b, w_down):
    s_ = x.shape[1]
    u = rmsnorm(x, norm_g) @ w_up
    up = jnp.pad(u, ((0, 0), (CONV_W - 1, 0), (0, 0)))
    c = conv_b + up[:, 0:s_] * conv_w[0]
    for j in range(1, CONV_W):
        c = c + up[:, j:j + s_] * conv_w[j]
    val, gate = jnp.split(c, 2, axis=-1)
    return (jax.nn.silu(gate) * val) @ w_down

def shared_kv(x, norm_g, w_kv, k_norm_g, cos, sin):
    b_, s_, _ = x.shape
    kv = rmsnorm(x, norm_g) @ w_kv
    k, v = jnp.split(kv, 2, axis=-1)
    k = apply_partial_rope(rmsnorm(k.reshape(b_, s_, A_HEADS, A_DH), k_norm_g), cos, sin)
    v = v.reshape(b_, s_, A_HEADS, A_DH)
    nb = -(-s_ // MOBA_BLOCK)
    pad = nb * MOBA_BLOCK - s_
    k = jnp.pad(k, ((0, 0), (0, pad), (0, 0), (0, 0)))
    v = jnp.pad(v, ((0, 0), (0, pad), (0, 0), (0, 0)))
    kb = k.reshape(b_, nb, MOBA_BLOCK, A_HEADS, A_DH).transpose(0, 3, 1, 2, 4)
    vb = v.reshape(b_, nb, MOBA_BLOCK, A_HEADS, A_DH).transpose(0, 3, 1, 2, 4)
    kmean = jnp.mean(kb.astype(jnp.float32), axis=3).astype(kb.dtype)
    return kb, vb, kmean

def moba_mixer(x, norm_g, w_q, q_norm_g, w_o, kb, vb, kmean, cos, sin):
    b_, s_, _ = x.shape
    q = (rmsnorm(x, norm_g) @ w_q).reshape(b_, s_, A_HEADS, A_DH)
    q = apply_partial_rope(rmsnorm(q, q_norm_g), cos, sin) * (A_DH ** -0.5)
    q = q.transpose(0, 2, 1, 3)
    nb = kb.shape[2]
    n_topk = min(MOBA_TOPK, nb)
    bidx = jnp.arange(b_)[:, None, None, None]
    hidx = jnp.arange(A_HEADS)[None, :, None, None]
    n_sel = n_topk * MOBA_BLOCK

    def attend_block(qi):
        start = qi * Q_BLOCK
        cur = start // MOBA_BLOCK
        qb = lax.dynamic_slice_in_dim(q, start, Q_BLOCK, axis=2)
        gate = jnp.einsum('bhqd,bhnd->bhqn', qb, kmean).astype(jnp.float32)
        gate = jnp.where(jnp.arange(nb) < cur, gate, -jnp.inf)
        _, sel = lax.top_k(gate, n_topk)
        sel_valid = jnp.arange(n_topk) < cur
        kg = kb[bidx, hidx, sel]
        vg = vb[bidx, hidx, sel]
        l_sel = jnp.einsum('bhqd,bhqjkd->bhqjk', qb, kg).astype(jnp.float32)
        l_sel = jnp.where(sel_valid[:, None], l_sel, -jnp.inf).reshape(b_, A_HEADS, Q_BLOCK, n_sel)
        ko = lax.dynamic_index_in_dim(kb, cur, axis=2, keepdims=False)
        vo = lax.dynamic_index_in_dim(vb, cur, axis=2, keepdims=False)
        l_own = jnp.einsum('bhqd,bhkd->bhqk', qb, ko).astype(jnp.float32)
        qpos = start + jnp.arange(Q_BLOCK)
        kpos = cur * MOBA_BLOCK + jnp.arange(MOBA_BLOCK)
        l_own = jnp.where(kpos[None, :] <= qpos[:, None], l_own, -jnp.inf)
        p = jax.nn.softmax(jnp.concatenate([l_sel, l_own], axis=-1), axis=-1).astype(vb.dtype)
        p_sel = p[..., :n_sel].reshape(b_, A_HEADS, Q_BLOCK, n_topk, MOBA_BLOCK)
        p_own = p[..., n_sel:]
        return jnp.einsum('bhqjk,bhqjkd->bhqd', p_sel, vg) + jnp.einsum('bhqk,bhkd->bhqd', p_own, vo)

    o = lax.map(attend_block, jnp.arange(s_ // Q_BLOCK))
    o = o.transpose(1, 0, 3, 2, 4).reshape(b_, s_, A_HEADS * A_DH)
    return o @ w_o

def first_inputs(seed: int = 0) -> dict:
    key = jax.random.key(seed)
    ks = jax.random.split(key, 20)
    f32 = jnp.float32

    def w(k, shape, fan_in, scale=1.0):
        return jax.random.normal(k, shape, f32) * (scale * fan_in ** -0.5)

    def gain(k, shape):
        return 1.0 + 0.05 * jax.random.normal(k, shape, f32)

    res_scale = (2 * DEPTH) ** -0.5
    gate_base = jnp.stack([jnp.zeros((M_HEADS,), f32), jnp.linspace(3.0, 6.0, M_HEADS, dtype=f32)])
    return {
        'x': jax.random.normal(ks[0], (BATCH, SEQ, D_MODEL), f32),
        'a_norm': gain(ks[1], (N_A, D_MODEL)),
        'a_w_in': w(ks[2], (N_A, D_MODEL, M_IN), D_MODEL),
        'a_b_gates': gate_base[None] + 0.1 * jax.random.normal(ks[3], (N_A, 2, M_HEADS), f32),
        'a_h_norm': gain(ks[4], (N_A, M_HEADS * M_DV)),
        'a_w_out': w(ks[5], (N_A, D_MODEL, D_MODEL), D_MODEL, res_scale),
        'kv_norm': gain(ks[6], (D_MODEL,)),
        'w_kv': w(ks[7], (D_MODEL, 2 * D_MODEL), D_MODEL),
        'k_norm': gain(ks[8], (A_DH,)),
        'b_norm': gain(ks[9], (N_B, D_MODEL)),
        'b_w_q': w(ks[10], (N_B, D_MODEL, D_MODEL), D_MODEL),
        'b_q_norm': gain(ks[11], (N_B, A_DH)),
        'b_w_o': w(ks[12], (N_B, D_MODEL, D_MODEL), D_MODEL, res_scale),
        'f_norm': gain(ks[13], (DEPTH, D_MODEL)),
        'f_w_up': w(ks[14], (DEPTH, D_MODEL, 2 * D_FF), D_MODEL),
        'f_conv_w': w(ks[15], (DEPTH, CONV_W, 2 * D_FF), CONV_W),
        'f_conv_b': 0.02 * jax.random.normal(ks[16], (DEPTH, 2 * D_FF), f32),
        'f_w_down': w(ks[17], (DEPTH, D_FF, D_MODEL), D_FF, res_scale),
    }

def first_block(x, a_norm, a_w_in, a_b_gates, a_h_norm, a_w_out, kv_norm, w_kv, k_norm,
              b_norm, b_w_q, b_q_norm, b_w_o, f_norm, f_w_up, f_conv_w, f_conv_b, f_w_down):
    cos, sin = rope_tables(x.shape[1])
    h = x
    kb = vb = kmean = None
    for l in range(DEPTH):
        if l < N_A:
            h = h + mlstm_mixer(h, a_norm[l], a_w_in[l], a_b_gates[l], a_h_norm[l], a_w_out[l])
        else:
            j = l - N_A
            h = h + moba_mixer(h, b_norm[j], b_w_q[j], b_q_norm[j], b_w_o[j], kb, vb, kmean, cos, sin)
        h = h + conv_ffn(h, f_norm[l], f_w_up[l], f_conv_w[l], f_conv_b[l], f_w_down[l])
        if l == N_A - 1:
            kb, vb, kmean = shared_kv(h, kv_norm, w_kv, k_norm, cos, sin)
    return h


D_CONV = 512
CONV_WIDTH = 31
N_HEADS = 8
D_HEAD_OUT = 64
D_ATTN = N_HEADS * D_HEAD_OUT
D_MIX = D_CONV + D_ATTN
Q_LORA = 256
KV_LORA = 128
N_IDX_HEADS = 8
D_IDX = 64
TOPK_MAX = 256
N_BUCKETS = 32
MAX_DISTANCE = 128
SPLIT_SIZES = (D_CONV, D_CONV, D_CONV, Q_LORA, KV_LORA, D_IDX, N_IDX_HEADS, D_ATTN)
D_IN_PROJ = sum(SPLIT_SIZES)


def rmsnorm_2(x, g):
    xf = x.astype(jnp.float32)
    y = xf * lax.rsqrt(jnp.mean(xf * xf, axis=-1, keepdims=True) + EPS)
    return (y * g.astype(jnp.float32)).astype(x.dtype)

def layernorm(x, g, b):
    xf = x.astype(jnp.float32)
    mu = jnp.mean(xf, axis=-1, keepdims=True)
    var = jnp.mean(jnp.square(xf - mu), axis=-1, keepdims=True)
    y = (xf - mu) * lax.rsqrt(var + EPS)
    return (y * g.astype(jnp.float32) + b.astype(jnp.float32)).astype(x.dtype)

def t5_bucket(n):
    max_exact = N_BUCKETS // 2
    n = jnp.maximum(n, 0)
    nf = jnp.maximum(n, 1).astype(jnp.float32)
    large = max_exact + (jnp.log(nf / max_exact) / math.log(MAX_DISTANCE / max_exact)
                         * (N_BUCKETS - max_exact)).astype(jnp.int32)
    large = jnp.minimum(large, N_BUCKETS - 1)
    return jnp.where(n < max_exact, n, large)

def conformer_conv(u_val, u_gate, conv_w, conv_b, ln_g, ln_b, w_pw2):
    a = u_val * jax.nn.sigmoid(u_gate)
    y = lax.conv_general_dilated(
        a, conv_w[:, None, :].astype(a.dtype), window_strides=(1,),
        padding=[(CONV_WIDTH - 1, 0)], dimension_numbers=("NWC", "WIO", "NWC"),
        feature_group_count=D_CONV) + conv_b
    y = jax.nn.silu(layernorm(y, ln_g, ln_b))
    return y @ w_pw2

def dsa_attention(c_q, c_kv, k_idx, w_idx, q_norm_g, w_uq, w_qidx, kv_norm_g, w_uv, rel_bias):
    B, L, _ = c_q.shape
    k_top = min(TOPK_MAX, L // 4)
    cq = rmsnorm_2(c_q, q_norm_g)
    q = (cq @ w_uq).reshape(B, L, N_HEADS, KV_LORA)
    q_idx = (cq @ w_qidx).reshape(B, L, N_IDX_HEADS, D_IDX)
    kv = rmsnorm_2(c_kv, kv_norm_g)
    w = w_idx.astype(jnp.float32) * (N_IDX_HEADS ** -0.5 * D_IDX ** -0.5)
    k_idx_f = k_idx.astype(jnp.float32)
    nb = L // Q_BLOCK
    key_pos = jnp.arange(L)

    def to_blocks(a):
        return a.reshape(B, nb, Q_BLOCK, *a.shape[2:]).swapaxes(0, 1)

    def block_fn(args):
        blk, q_b, qi_b, w_b = args
        t_pos = blk * Q_BLOCK + jnp.arange(Q_BLOCK)
        s_raw = jnp.einsum("bthd,bsd->bths", qi_b.astype(jnp.float32), k_idx_f)
        score = jnp.einsum("bth,bths->bts", w_b, jax.nn.relu(s_raw))
        causal = key_pos[None, :] <= t_pos[:, None]
        score = jnp.where(causal[None], score, -jnp.inf)
        _, sel = lax.top_k(score, k_top)
        kv_sel = jax.vmap(lambda kv_b, i_b: kv_b[i_b])(kv, sel)
        logits = jnp.einsum("bthc,btkc->bthk", q_b, kv_sel).astype(jnp.float32) * (KV_LORA ** -0.5)
        dist = t_pos[None, :, None] - sel
        bias = jnp.moveaxis(rel_bias[t5_bucket(dist)], -1, 2)
        logits = logits + bias.astype(jnp.float32)
        valid = (dist >= 0)[:, :, None, :]
        probs = jax.nn.softmax(jnp.where(valid, logits, -jnp.inf), axis=-1)
        return jnp.einsum("bthk,btkc->bthc", probs.astype(kv.dtype), kv_sel)

    o = lax.map(block_fn, (jnp.arange(nb), to_blocks(q), to_blocks(q_idx), to_blocks(w)))
    o = o.swapaxes(0, 1).reshape(B, L, N_HEADS, KV_LORA)
    o = jnp.einsum("bshc,hcd->bshd", o, w_uv)
    return o.reshape(B, L, D_ATTN)

def second_inputs(seed: int = 0) -> dict:
    key = jax.random.key(seed)
    ks = jax.random.split(key, 24)
    f32 = jnp.float32
    nrm = lambda k, shape, s: jax.random.normal(k, shape, f32) * s
    return {
        "x": nrm(ks[0], (BATCH, SEQ, D_MODEL), 1.0),
        "c": nrm(ks[1], (BATCH, D_MODEL), 1.0),
        "w_ada": nrm(ks[2], (DEPTH, D_MODEL, 3 * D_MODEL), D_MODEL ** -0.5),
        "b_ada": nrm(ks[3], (DEPTH, 3 * D_MODEL), 0.02),
        "g_pre": 1.0 + nrm(ks[4], (DEPTH, D_MODEL), 0.05),
        "w_in": nrm(ks[5], (DEPTH, D_MODEL, D_IN_PROJ), D_MODEL ** -0.5),
        "conv_w": nrm(ks[6], (DEPTH, CONV_WIDTH, D_CONV), CONV_WIDTH ** -0.5),
        "conv_b": nrm(ks[7], (DEPTH, D_CONV), 0.02),
        "conv_ln_g": 1.0 + nrm(ks[8], (DEPTH, D_CONV), 0.05),
        "conv_ln_b": nrm(ks[9], (DEPTH, D_CONV), 0.02),
        "w_pw2": nrm(ks[10], (DEPTH, D_CONV, D_CONV), D_CONV ** -0.5),
        "q_norm_g": 1.0 + nrm(ks[11], (DEPTH, Q_LORA), 0.05),
        "w_uq": nrm(ks[12], (DEPTH, Q_LORA, N_HEADS * KV_LORA), Q_LORA ** -0.5),
        "w_qidx": nrm(ks[13], (DEPTH, Q_LORA, N_IDX_HEADS * D_IDX), Q_LORA ** -0.5),
        "kv_norm_g": 1.0 + nrm(ks[14], (DEPTH, KV_LORA), 0.05),
        "w_uv": nrm(ks[15], (DEPTH, N_HEADS, KV_LORA, D_HEAD_OUT), KV_LORA ** -0.5),
        "rel_bias": nrm(ks[16], (N_BUCKETS, N_HEADS), 0.5),
        "w_out": nrm(ks[17], (DEPTH, D_MIX, D_MODEL), D_MIX ** -0.5),
        "g_post": 1.0 + nrm(ks[18], (DEPTH, D_MODEL), 0.05),
    }

def second_block(x, c, w_ada, b_ada, g_pre, w_in, conv_w, conv_b, conv_ln_g, conv_ln_b, w_pw2,
              q_norm_g, w_uq, w_qidx, kv_norm_g, w_uv, rel_bias, w_out, g_post):
    offsets = [int(v) for v in np.cumsum(SPLIT_SIZES)[:-1]]
    c_act = jax.nn.silu(c)
    for l in range(DEPTH):
        mod = c_act @ w_ada[l] + b_ada[l]
        shift, scale, gate = jnp.split(mod, 3, axis=-1)
        h = rmsnorm_2(x, g_pre[l]) * (1.0 + scale[:, None, :]) + shift[:, None, :]
        p = h @ w_in[l]
        u_val, u_gate, g_conv, c_q, c_kv, k_idx, w_idx, g_attn = jnp.split(p, offsets, axis=-1)
        y_conv = conformer_conv(u_val, u_gate, conv_w[l], conv_b[l], conv_ln_g[l], conv_ln_b[l],
                                w_pw2[l]) * jax.nn.silu(g_conv)
        y_attn = dsa_attention(c_q, c_kv, k_idx, w_idx, q_norm_g[l], w_uq[l], w_qidx[l],
                               kv_norm_g[l], w_uv[l], rel_bias) * jax.nn.silu(g_attn)
        y = jnp.concatenate([y_conv, y_attn], axis=-1) @ w_out[l]
        x = x + gate[:, None, :] * rmsnorm_2(y, g_post[l])
    return x


def setup_inputs(seed=0):
    out = dict(first_inputs(seed))
    for name, value in second_inputs(seed + 1).items():
        if name != "x":
            out[name + "_2"] = value
    return out


def reference(
    x, a_norm, a_w_in, a_b_gates, a_h_norm, a_w_out, kv_norm, w_kv, k_norm, b_norm, b_w_q,
    b_q_norm, b_w_o, f_norm, f_w_up, f_conv_w, f_conv_b, f_w_down, c_2, w_ada_2, b_ada_2,
    g_pre_2, w_in_2, conv_w_2, conv_b_2, conv_ln_g_2, conv_ln_b_2, w_pw2_2, q_norm_g_2, w_uq_2,
    w_qidx_2, kv_norm_g_2, w_uv_2, rel_bias_2, w_out_2, g_post_2,
):
    x = first_block(
        x, a_norm, a_w_in, a_b_gates, a_h_norm, a_w_out, kv_norm, w_kv, k_norm, b_norm, b_w_q,
        b_q_norm, b_w_o, f_norm, f_w_up, f_conv_w, f_conv_b, f_w_down,
    )
    return second_block(
        x, c_2, w_ada_2, b_ada_2, g_pre_2, w_in_2, conv_w_2, conv_b_2, conv_ln_g_2, conv_ln_b_2,
        w_pw2_2, q_norm_g_2, w_uq_2, w_qidx_2, kv_norm_g_2, w_uv_2, rel_bias_2, w_out_2,
        g_post_2,
    )


_drawn_inputs = setup_inputs


def setup_inputs(seed=0):
    import zlib

    import numpy as np

    out = dict(_drawn_inputs(seed))
    spreads = {}
    factors = {'kv_norm': 3.752,
     'k_norm': 4.663,
     'b_norm': 5.331,
     'b_q_norm': 4.8,
     'f_conv_b': 2.697,
     'conv_b_2': 3.037,
     'conv_ln_b_2': 4.277,
     'conv_ln_g_2': 2.87,
     'q_norm_g_2': 3.891,
     'kv_norm_g_2': 4.371,
     'g_post_2': 2.717}
    for name, (base, spread) in spreads.items():
        noise = np.random.default_rng([zlib.crc32(name.encode()), seed]).standard_normal(out[name].shape)
        drawn = base * np.exp(spread * noise) if base else spread * noise
        out[name] = __import__('jax').numpy.asarray(drawn.astype(out[name].dtype))
    for name, factor in factors.items():
        out[name] = (out[name] * factor).astype(out[name].dtype)
    return out
```

```python
from contextlib import ExitStack

import numpy as np

import concourse.bass as bass
from concourse import mybir

F32 = mybir.dt.float32
ALU = mybir.AluOpType
ACT = mybir.ActivationFunctionType
AX = mybir.AxisListType

P = 128
T = 256
TB = T // P
D = 1024
DC = D // P
EPS = 1e-6
M_HEADS, M_DQK, M_DV = 4, 128, 256
A_HEADS, A_DH = 8, 128
ROT = A_DH // 4
HALF = ROT // 2
D_FF = 2816
FF_STEPS = D_FF // 256
DEPTH = 2
D_CONV, TAPS = 512, 31
CC = D_CONV // P
IDX_HEADS, D_IDX = 8, 64
KV_LORA = 128
TOPK = 64
IDX_ORDER = ((0, 2), (1, 3), (4, 6), (5, 7), (0, 2, 4, 6), (1, 3, 5, 7))
BUCKETS, MAX_DISTANCE = 32, 128
NEG = -1e30
CAUSAL = -3.0e38
PICKED = -3.4e38
RING = 8
DIAG = P + T

COLS = {}
_n = 0
for _name, _rows in ([("f_conv_w0", 132), ("f_conv_b0", 44), ("f_conv_w1", 132), ("f_conv_b1", 44),
                      ("a_norm", 8), ("f_norm", 16), ("kv_norm", 8), ("b_norm", 8), ("a_h_norm", 8),
                      ("k_norm", 1), ("b_q_norm", 1), ("c_2", 8), ("b_ada_2", 48), ("g_pre_2", 16),
                      ("conv_w_2", 248), ("conv_b_2", 8), ("conv_ln_g_2", 8), ("conv_ln_b_2", 8),
                      ("q_norm_g_2", 4), ("kv_norm_g_2", 2), ("g_post_2", 16)]):
    COLS[_name] = (_n, _rows)
    _n += _rows
NCOL = -(-_n // P) * P
PIECES = []
for _name, (_at, _rows) in COLS.items():
    _done = 0
    while _done < _rows:
        _m = min(_rows - _done, P - (_at + _done) % P)
        PIECES.append((_name, _done, _at + _done, _m))
        _done += _m
NTURN = NCOL // P

CONST = {}
_n = 0
for _name, _w in (("ident", P), ("flip", P), ("mask_st", T), ("mask_ts", DIAG), ("mask_top", DIAG),
                  ("cos", TB * HALF), ("sin", TB * HALF), ("head_col", 16), ("head_row", 4 * P),
                  ("bucket", 3 * P)):
    CONST[_name] = (_n, _w)
    _n += _w
NCONST = _n


def shape_constants():
    c = np.zeros((P, NCONST), np.float32)

    def put(name, a):
        c[:a.shape[0], CONST[name][0]:CONST[name][0] + a.shape[1]] = a

    p = np.arange(P)
    put("ident", np.eye(P, dtype=np.float32))
    put("flip", np.eye(P, dtype=np.float32)[::-1])
    later = np.where(p[None, :] < p[:, None], NEG, 0.0)
    put("mask_st", np.concatenate([later, np.zeros((P, P))], 1))
    ahead = p[None, :] > p[:, None]
    for name, v in (("mask_ts", NEG), ("mask_top", CAUSAL)):
        m = np.where(ahead, v, 0.0)
        put(name, np.concatenate([m, np.zeros((P, P)), m], 1))
    inv = np.float32(500000.0) ** (-np.arange(0, ROT, 2, dtype=np.float32) / np.float32(ROT))
    ang = np.arange(T, dtype=np.float32)[:, None] * inv.astype(np.float32)[None, :]
    for name, f in (("cos", np.cos), ("sin", np.sin)):
        t = f(ang).astype(np.float32).reshape(TB, P, HALF)
        put(name, t.transpose(1, 0, 2).reshape(P, TB * HALF))
    hc = np.zeros((P, 4, 4))
    hr = np.zeros((4, 4, P))
    for h in range(4):
        hc[:, h, h] = 1
        hr[h, h, :] = 1
    put("head_col", hc.reshape(P, 16))
    put("head_row", hr.reshape(4, 4 * P))
    dist = np.maximum(T - 1 - np.arange(3 * P), 0)
    exact = BUCKETS // 2
    near = np.maximum(dist, 1).astype(np.float32)
    large = exact + (np.log(near / np.float32(exact)) / np.float32(np.log(MAX_DISTANCE / exact))
                     * np.float32(BUCKETS - exact)).astype(np.int32)
    bucket = np.where(dist < exact, dist, np.minimum(large, BUCKETS - 1))
    put("bucket", (np.arange(BUCKETS)[:, None] == bucket[None, :]).astype(np.float32))
    return c


def model(nc, I, out):
    with ExitStack() as ctx:
        def sb(name, shape):
            return ctx.enter_context(nc.sbuf_tensor(name, shape, F32))

        sems = {}

        def S(name):
            if name not in sems:
                sems[name] = ctx.enter_context(nc.semaphore(name))
            return sems[name]

        ring = sb("ring", [P, RING, 2048])
        fring = sb("fring", [P, 2, 3, 2048])
        work = sb("work", [P, 6 * 2048])
        hT = sb("hT", [P, DC, T])
        xg = sb("xg", [P, DC, T])
        sq = sb("sq", [P, DC, T])
        consts = sb("consts", [P, NCONST])
        cols = sb("cols", [P, NCOL])
        ones = sb("ones", [P, T])
        ms = sb("ms", [P, 2 * T])
        lny = sb("lny", [P, 2 * T])
        nwt = sb("nwt", [P, 2 * T])
        rstd = sb("rstd", [P, 2 * T])
        rcol = sb("rcol", [P, TB])
        sml = sb("sml", [P, 192])
        mod = sb("mod", [P, DEPTH, 24])
        cact = sb("cact", [P, 8])
        pb = [ctx.enter_context(nc.psum_tensor(f"bank{i}", [P, 512], F32)) for i in range(8)]

        def W(a, b):
            return work[:, a:b]

        def pc(name, w, at=0):
            a = CONST[name][0] + at
            return consts[:, a:a + w]

        def col(name, i):
            return cols[:, bass.ds(COLS[name][0] + i, 1)]

        def three(ap, n):
            return ap.rearrange("p (a b) -> p a b", a=n)

        ident = pc("ident", P)
        rbc = rstd[:, 0:T]
        rbc2 = rbc.unsqueeze(1).broadcast_to([P, 2, T])

        m_q, m_k = three(W(0, 1024), 4), three(W(1024, 2048), 4)
        m_v = three(W(2048, 4096), TB)
        m_o = three(W(4096, 6144), DC)
        m_num = three(W(6144, 8192), DC)
        m_gw = W(8192, 8704).rearrange("p (k n) -> p k n", k=DC)
        m_e = [W(8704 + 384 * i, 9088 + 384 * i) for i in range(2)]
        m_pt = [W(9472 + 384 * i, 9856 + 384 * i) for i in range(2)]
        m_y = xg
        m_sqn = sq[:, 0:4, :]
        rows = W(9856, 11904)[0:36, :].rearrange("p (a t) -> p a t", a=8)
        scratch = nc.dram_tensor("bias_rows", (8, 3 * P), F32)
        pstage = three(W(0, NCOL), NTURN)
        a_xq = three(W(0, 2048), DC)
        a_qT = three(W(0, 2048), 8)
        a_kt, a_qt = three(W(2048, 4096), TB), three(W(4096, 6144), TB)
        a_v = three(W(6144, 8192), TB)
        a_kT = three(W(8192, 10240), 8)
        a_oT = three(W(10240, 12288), 8)
        a_sq = W(10240, 12288)
        a_rot = [W(10240 + 256 * i, 10496 + 256 * i).rearrange("p (b h d) -> p b h d", b=TB, h=8)
                 for i in range(4)]
        f_ada = three(W(0, 3072), 2)
        f_acc = W(3072, 6144)
        f_act = three(W(6144, 7168), 2)
        f_t = [three(W(7168 + 512 * i, 7680 + 512 * i), 2) for i in range(2)]
        f_u = W(8192, 8192 + 4 * 258).rearrange("p (g c t) -> p g c t", g=2, c=2)
        f_sg = W(9300, 9812)
        sqf = sq[:, :, :].rearrange("p a b -> p (a b)")
        sc_sb = [sqf[:, DIAG * i:DIAG * (i + 1)] for i in range(2)]
        p_sb = [sqf[:, DIAG * (2 + i):DIAG * (3 + i)] for i in range(2)]
        pt_sb = [sqf[:, DIAG * 4:DIAG * 5], nwt[:, 0:DIAG]]
        x_rows = three(sqf, TB)
        y_rows = x_rows
        fr = fring[:, :, :, :].rearrange("p a b c -> p (a b c)")
        biasT = fr[:, 0:3072].rearrange("p (h t) -> p h t", h=8)
        skew = fr[:, 3072:5120].rearrange("p (h t) -> p h t", h=8)
        y2 = three(fr[:, 5120:7168], DC)
        small_w = fr[:, 7168:7168 + 1088 + 512]
        w_widx = small_w[:, 0:64].rearrange("p (k n) -> p k n", k=DC)
        w_qidx = small_w[:, 64:1088].rearrange("p (k n) -> p k n", k=2)
        w_uv = small_w[:, 1088:1600].rearrange("p (h n) -> p h n", h=8)
        am = [fr[:, 8768 + DIAG * i:8768 + DIAG * (i + 1)] for i in range(2)]
        kmask = fr[:, 9536:9536 + DIAG]
        ts = fr[:, 9920:9920 + DIAG]
        relu = [fr[:, 10304 + 512 * i:10816 + 512 * i] for i in range(2)]
        wcol = fr[:, 11328:11344].rearrange("p (a b) -> p a b", a=TB)
        best = fr[:, 11344:11360].rearrange("p (a b) -> p a b", a=TB)
        widx_row = fr[:, 11360:11616]
        b_cq = three(W(0, 512), 2)
        b_kv = W(512, 768)
        b_kidx = W(768, 1024)
        b_cqn = three(W(1024, 1536), 2)
        b_kvn = W(1536, 1792)
        b_kvt = three(W(1792, 2048), TB)
        b_qT = three(W(2048, 4096), 8)
        b_qi = three(W(4096, 5120), 4)
        b_yn = three(W(5120, 6144), CC)
        b_a = W(6144, 6144 + CC * (T + TAPS - 1)).rearrange("p (c t) -> p c t", c=CC)
        b_y = three(W(7300, 8324), CC)
        b_z = three(W(8324, 9348), CC)
        b_sg = three(W(9348, 9860), 2)
        b_oT = three(W(10240, 12288), 8)
        b_yT = b_qT

        def cut(w, c, n=256):
            return w.rearrange("(k p) n -> p k n", p=P)[:, :, c:c + n]

        def slot(n):
            return ring[:, n % RING, :]

        def slot8(n):
            return slot(n).rearrange("p (k n) -> p k n", k=8)

        HQ = M_HEADS * M_DQK
        loads = [[(slot8(n), cut(I["a_w_in"][0], 256 * n))] for n in range(12)]
        loads += [[(slot8(n), cut(I["a_w_out"][0], 256 * (n - 12)))] for n in range(12, 16)]
        loads += [[(slot8(n), cut(I["w_kv"], 256 * (n - 16)))] for n in range(16, 20)]
        loads += [[(slot8(n), cut(I["b_w_q"][0], 256 * (n - 20)))] for n in range(20, 24)]
        loads += [[(slot8(n), cut(I["w_kv"], D + 256 * (n - 24)))] for n in range(24, 28)]
        loads += [[(slot8(n), cut(I["b_w_o"][0], 256 * (n - 28)))] for n in range(28, 32)]
        O_VAL, O_GATE, O_GC, O_CQ, O_KV, O_KI, O_WI, O_GA = 0, 512, 1024, 1536, 1792, 1920, 1984, 1992
        for l in range(DEPTH):
            n = 32 + 16 * l
            w = I["w_in_2"][l]
            loads.append([(slot8(n), cut(w, O_CQ))])
            s = slot8(n + 1)
            loads.append([(s[:, :, 0:192], cut(w, O_KV, 192)), (s[:, :, 192:256], cut(w, O_KI, 64))])
            for i, c in ((2, O_VAL), (3, O_GATE)):
                loads.append([(slot8(n + i), cut(w, c))])
            loads.append([(slot(n + 4).rearrange("p (k n) -> p k n", k=2),
                           I["w_uq_2"][l].rearrange("(k p) n -> p k n", p=P))])
            for i, c in enumerate((O_VAL + 256, O_GATE + 256, O_GC, O_GC + 256, O_GA, O_GA + 256)):
                loads.append([(slot8(n + 5 + i), cut(w, c))])
            loads.append([(slot(n + 11).rearrange("p (k n) -> p k n", k=CC),
                           I["w_pw2_2"][l].rearrange("(k p) n -> p k n", p=P))])
            loads += [[(slot8(n + 12 + i), cut(I["w_out_2"][l], 256 * i))] for i in range(4)]
        landed = [0] * RING
        ring_count = []
        for n, parts in enumerate(loads):
            landed[n % RING] += 16 * len(parts)
            ring_count.append(landed[n % RING])

        def arrived(eng, n):
            eng.wait_ge(S(f"ring{n % RING}"), ring_count[n])

        def product(eng, n):
            eng.wait_ge(S("product"), n + 1)

        block = ctx.enter_context(nc.Block())

        @block.sync
        def _(sp):
            def load(n):
                if n >= RING:
                    product(sp, n - RING)
                for dst, src in loads[n]:
                    sp.dma_start(dst, src).then_inc(S(f"ring{n % RING}"), 16)

            def load_ffn(f, i, par, first):
                up = I["f_w_up"][f].rearrange("(k p) n -> p k n", p=P)
                down = I["f_w_down"][f].rearrange("(k p) n -> p k n", p=P)
                g = FF_STEPS * f + i
                if not first:
                    sp.wait_ge(S("up_done"), g - 1)
                for j, c in enumerate((i * 256, D_FF + i * 256)):
                    sp.dma_start(fring[:, par, j, :].rearrange("p (k n) -> p k n", k=8),
                                 up[:, :, bass.ds(c, 256)]).then_inc(S(f"f_up{par}"), 16)
                if not first:
                    sp.wait_ge(S("down_done"), g - 1)
                sp.dma_start(fring[:, par, 2, :].rearrange("p (k n) -> p k n", k=2),
                             down[:, bass.ds(2 * i, 2), :]).then_inc(S(f"f_down{par}"), 16)

            def load_ada(l, k):
                src = I["w_ada_2"][l].rearrange("(k p) n -> p k n", p=P)
                for half in range(2):
                    sp.wait_ge(S("ada_free"), 2 * (8 * l + k) + half + 1)
                    sp.dma_start(f_ada[:, half, :].unsqueeze(1),
                                 src[:, bass.ds(k, 1), 1536 * half:1536 * half + 1536])\
                        .then_inc(S(f"ada{half}"), 16)

            def ffn_loads(f):
                sp.wait_ge(S("up_done"), FF_STEPS * f + 1)
                with sp.Fori(0, 4) as j:
                    for s in range(2):
                        load_ffn(f, 2 * j + s + 2, (FF_STEPS * f + s) % 2, False)
                        load_ada(f, 2 * j + s)
                load_ffn(f, FF_STEPS - 1, (FF_STEPS * f + FF_STEPS - 1) % 2, False)

            for n in range(RING):
                if n == 2:
                    sp.wait_ge(S("param_in"), 16 * len(PIECES))
                load(n)
            load_ffn(0, 0, 0, True)
            load_ffn(0, 1, 1, True)
            for n in range(8, 24):
                load(n)
            ffn_loads(0)
            load_ffn(1, 0, 1, False)
            load_ffn(1, 1, 0, False)
            for n in range(24, 40):
                load(n)
            ffn_loads(1)
            sp.wait_ge(S("down_done"), 2 * FF_STEPS)
            sp.wait_ge(S("rows_out"), 16)
            sp.dma_start(skew, bass.AP(scratch, 0, [[1, P], [3 * P, 8], [1, T]])).then_inc(S("skew_in"), 16)
            for l in range(DEPTH):
                if l > 0:
                    sp.wait_ge(S("uv_done"), 2 * l)
                w = I["w_in_2"][l].rearrange("(k p) n -> p k n", p=P)
                sp.dma_start(w_widx, w[:, :, O_WI:O_WI + 8]).then_inc(S("small_in"), 16)
                sp.dma_start(w_qidx, I["w_qidx_2"][l].rearrange("(k p) n -> p k n", p=P))\
                    .then_inc(S("small_in"), 16)
                sp.dma_start(w_uv, I["w_uv_2"][l].rearrange("h p n -> p h n")).then_inc(S("small_in"), 16)
                for n in (range(40, 48) if l == 0 else range(48, 64)):
                    load(n)
            sp.wait_ge(S("y_cp"), 4)
            sp.dma_start(out[0].rearrange("(b p) n -> p b n", p=P), y_rows).then_inc(S("stored"), 16)
            sp.wait_ge(S("stored"), 16)

        @block.gpsimd
        def _(pool):
            nc.gpsimd.memset(ones[:, :], 1.0).then_inc(S("ones_set"), 1)
            nc.gpsimd.memset(m_gw[:, :, :], 0.0).then_inc(S("gw_zero"), 1)
            for l in range(DEPTH):
                for h in range(8):
                    n = 8 * l + h
                    pool.wait_ge(S("kmask_done"), l + 1)
                    if h == 0:
                        pool.wait_ge(S("bias_cp"), 8)
                    if n >= 2:
                        pool.wait_ge(S("max_done"), 8 + n - 1)
                    nc.gpsimd.tensor_tensor(am[h % 2], biasT[:, h, :], kmask, ALU.add)\
                        .then_inc(S("am_done"), 1)

        @block.scalar
        def _(act):
            done = [0]

            def link(ins):
                done[0] = done[0] + 1
                ins.then_inc(S("act_step"), 1)
                return done[0]

            def after(n):
                act.wait_ge(S("act_step"), n)

            def root(nn, src, tmp, dst):
                act.wait_ge(S("ms_done"), nn + 1)
                if nn >= 1:
                    act.wait_ge(S("rstd_done"), nn)
                after(link(nc.scalar.activation(tmp, src, ACT.Ln)))
                nc.scalar.activation(dst, tmp, ACT.Exp, scale=-0.5).then_inc(S("guess_done"), 1)

            def squares(k):
                for half in range(2):
                    act.wait_ge(S("h_ready"), 2 * k + half + 1)
                    nc.scalar.activation(sq[:, 4 * half:4 * half + 4, :], hT[:, 4 * half:4 * half + 4, :],
                                         ACT.Square).then_inc(S("sq_done"), 1)

            act.dma_start(x_rows[:, 0, :], I["x"][0, 0:P, :]).then_inc(S("x_in"), 16)
            act.dma_start(x_rows[:, 1, :], I["x"][0, P:T, :]).then_inc(S("x_in"), 16)
            act.dma_start(consts[:, :], I["consts"]).then_inc(S("const_in"), 16)
            flat = {"f_conv_w0": I["f_conv_w"][0].rearrange("j (c p) -> j c p", p=P),
                    "f_conv_w1": I["f_conv_w"][1].rearrange("j (c p) -> j c p", p=P),
                    "f_conv_b0": I["f_conv_b"][0].rearrange("(c p) -> c p", p=P),
                    "f_conv_b1": I["f_conv_b"][1].rearrange("(c p) -> c p", p=P)}
            for name, first, r, m in PIECES:
                src = I[name] if name in I else flat[name]
                if name in ("kv_norm", "k_norm"):
                    src = src.rearrange("(c p) -> c p", p=P)
                elif name == "conv_w_2":
                    src = src.rearrange("l j (c p) -> (l j c) p", p=P)
                elif name in I:
                    src = src.rearrange("l (c p) -> (l c) p", p=P)
                elif "conv_w" in name:
                    src = src.rearrange("j c p -> (j c) p")
                act.dma_start(pstage[r % P:r % P + m, r // P, :], src[first:first + m, :])\
                    .then_inc(S("param_in"), 16)
            act.wait_ge(S("gw_zero"), 1)
            w = I["a_w_in"][0].rearrange("(k p) n -> p k n", p=P)
            act.dma_start(m_gw[:, :, 0:4], w[:, :, 3072:3076]).then_inc(S("gw_in"), 16)
            act.dma_start(m_gw[:, :, 32:36], w[:, :, 3076:3080]).then_inc(S("gw_in"), 16)
            act.dma_start(sml[0:4, 160:161], I["a_b_gates"][0, 0, :].unsqueeze(1)).then_inc(S("gb_in"), 16)
            act.dma_start(sml[32:36, 160:161], I["a_b_gates"][0, 1, :].unsqueeze(1)).then_inc(S("gb_in"), 16)
            act.dma_start(sml[0:BUCKETS, 161:169], I["rel_bias_2"]).then_inc(S("rb_in"), 16)
            act.dma_start(sml[:, 64:96], I["k_norm"][0:ROT].partition_broadcast(P)).then_inc(S("gbc_in"), 16)
            act.dma_start(sml[:, 96:128], I["b_q_norm"][0, 0:ROT].partition_broadcast(P)).then_inc(S("gbc_in"), 16)
            act.wait_ge(S("params_turned"), 2)
            nc.scalar.activation(cols[:, 0:512], pb[4][:, :], ACT.Copy).then_inc(S("cols_done"), 1)
            nc.scalar.activation(cols[:, 512:NCOL], pb[5][:, 0:NCOL - 512], ACT.Copy)\
                .then_inc(S("cols_done"), 1)

            squares(0)
            act.wait_ge(S("rowsT_done"), 1)
            nc.scalar.activation(work[0:8, 11904:12288], pb[6][0:8, 0:3 * P], ACT.Copy)\
                .then_inc(S("rows_done"), 1)
            act.wait_ge(S("rows_done"), 1)
            act.dma_start(scratch.ap(), work[0:8, 11904:12288]).then_inc(S("rows_out"), 16)
            root(0, ms[:, 0:T], lny[:, 0:T], rstd[:, 0:T])
            act.wait_ge(S("fabs_done"), 1)
            after(link(nc.scalar.activation(rows[32:36, 2, :], rows[32:36, 1, :], ACT.Exp, scale=-1.0)))
            nc.scalar.activation(rows[32:36, 3, :], rows[32:36, 2, :], ACT.Ln, bias=1.0)\
                .then_inc(S("fln_done"), 1)
            for s in range(4):
                product(act, 4 + s)
                if s == 0:
                    act.wait_ge(S("rcol_done"), 1)
                for b in range(TB):
                    nc.scalar.activation(m_v[:, b, 256 * s:256 * s + 256], pb[(6 + s) % 8][:, 256 * b:256 * b + 256],
                                         ACT.Copy, scale=rcol[:, b:b + 1]).then_inc(S("m_v_out"), 1)
            act.wait_ge(S("m_rows_done"), 1)
            nc.scalar.activation(rows[0:4, 3, :], rows[0:4, 2, :], ACT.Exp, scale=-1.0)\
                .then_inc(S("floor_done"), 1)

            def decay(h):
                act.wait_ge(S("m_tmp"), h + 1)
                if h == 0:
                    act.wait_ge(S("ccol_done"), 1)
                e = m_e[h % 2]
                nc.scalar.activation(e[:, 0:T], e[:, 0:T], ACT.Exp, bias=sml[:, h:h + 1])\
                    .then_inc(S("m_exp"), 1)
                nc.scalar.activation(e[:, T:DIAG], e[:, T:DIAG], ACT.Exp, bias=sml[:, 4 + h:5 + h])\
                    .then_inc(S("m_exp"), 1)

            def numer(h):
                act.wait_ge(S("m_num_done"), h + 1)
                bank = pb[h % 2][:, :].rearrange("p (a b) -> p a b", a=2)
                nc.scalar.activation(m_num[:, 2 * h:2 * h + 2, :], bank, ACT.Copy).then_inc(S("m_num_out"), 1)
                if h >= 2:
                    act.wait_ge(S("m_sqs"), h - 1)
                nc.scalar.activation(m_sqn[:, 2 * (h % 2):2 * (h % 2) + 2, :], bank, ACT.Square)\
                    .then_inc(S("m_num_out"), 1)

            decay(0)
            for h in range(4):
                if h < 3:
                    decay(h + 1)
                numer(h)
            root(1, rows[0:4, 5, :], rows[0:4, 6, :], rows[0:4, 7, :])
            for h in range(4):
                act.wait_ge(S("m_o_scaled"), h + 1)
                nc.scalar.activation(m_o[:, 2 * h:2 * h + 2, :], m_o[:, 2 * h:2 * h + 2, :], ACT.Sigmoid)\
                    .then_inc(S("m_o_gate"), 1)

            def ffn(f):
                def step(g, i, par):
                    act.wait_ge(S("u_ready"), g + 1)
                    act.wait_ge(S("act_ready"), g)
                    for v in range(2):
                        for c in range(2):
                            n = 22 * v + 2 * i + c
                            nc.scalar.activation(f_t[v][:, c, :], f_u[:, v, c, 0:T], ACT.Identity,
                                                 bias=col(f"f_conv_b{f}", n),
                                                 scale=col(f"f_conv_w{f}", n)).then_inc(S("tap0_done"), 1)
                    act.wait_ge(S("gate_conv"), g + 1)
                    nc.scalar.activation(f_sg.rearrange("p (a b) -> p a b", a=2), f_t[1], ACT.Silu)\
                        .then_inc(S("silu_done"), 1)

                g0 = FF_STEPS * f
                for i in (0, 1):
                    step(g0 + i, i, (g0 + i) % 2)
                with act.Fori(0, 4) as j:
                    for s in range(2):
                        i = 2 * j + s + 2
                        step(g0 + i, i, (g0 + s) % 2)
                step(g0 + FF_STEPS - 1, FF_STEPS - 1, (g0 + FF_STEPS - 1) % 2)

            squares(1)
            root(2, ms[:, 0:T], lny[:, 0:T], rstd[:, 0:T])
            nc.scalar.activation(cact[:, :], cols[:, COLS["c_2"][0]:COLS["c_2"][0] + 8], ACT.Silu)\
                .then_inc(S("cact_done"), 1)
            ffn(0)

            squares(2)
            root(3, ms[:, 0:T], lny[:, 0:T], rstd[:, 0:T])
            banks = [0, 1, 2, 3, 4, 5, 6, 0, 1, 2, 3, 4]

            def rows_out(s):
                product(act, 16 + s)
                dst = (a_kt, a_qt, a_v)[s // 4]
                for b in range(TB):
                    c = 256 * (s % 4)
                    nc.scalar.activation(dst[:, b, c:c + 256], pb[banks[s]][:, 256 * b:256 * b + 256],
                                         ACT.Copy, scale=rcol[:, b:b + 1]).then_inc(S("tok_out"), 1)

            def head_squares(i):
                act.wait_ge(S("tok_out"), 8 * (i + 1))
                if i == 0:
                    act.wait_ge(S("rows_out"), 16)
                if i == 1:
                    act.wait_ge(S("rot_done"), 1)
                src = (a_kt, a_qt)[i]
                nc.scalar.activation(a_sq, src.rearrange("p a b -> p (a b)"), ACT.Square)\
                    .then_inc(S("hsq_done"), 1)
                root(4 + i, sml[:, 0:16], sml[:, 16:32], sml[:, 32:48])

            act.wait_ge(S("rcol_done"), 2)
            for s in range(4):
                rows_out(s)
            head_squares(0)
            for s in range(4, 8):
                rows_out(s)
            head_squares(1)
            for s in range(8, 12):
                rows_out(s)
            for i, dst in ((0, a_kT), (1, a_qT)):
                for m in range(4):
                    act.wait_ge(S("a_turned"), 4 * i + m + 1)
                    nc.scalar.activation(dst[:, 2 * m:2 * m + 2, :],
                                         three(pb[(5, 6, 7, 0, 1, 2, 3, 4)[4 * i + m]][:, :], 2),
                                         ACT.Copy, scale=sml[:, 128 + i:129 + i]).then_inc(S("turn_out"), 1)

            def attention(a, oT, gate=None):
                for n in range(10):
                    if n < 8:
                        h = 8 * a + n
                        act.wait_ge(S("max_done"), h + 1)
                        for b, (x, y) in enumerate(((0, P), (P, DIAG))):
                            at = 136 + 2 * (n % 2) + b
                            nc.scalar.activation(p_sb[n % 2][:, x:y], sc_sb[n % 2][:, x:y], ACT.Exp,
                                                 scale=-1.0, bias=sml[:, at:at + 1],
                                                 accum_out=sml[:, at + 4:at + 5])\
                                .then_inc(S("exp_done"), 1)
                    if gate is not None and n < 9:
                        gate(n)
                    if 1 <= n < 9:
                        h = 8 * a + n - 1
                        act.wait_ge(S("p_turned"), h + 1)
                        nc.scalar.activation(pt_sb[(n - 1) % 2], pb[2 + (n - 1) % 2][:, 0:DIAG], ACT.Copy)\
                            .then_inc(S("pt_out"), 1)
                    if n >= 2:
                        h = 8 * a + n - 2
                        act.wait_ge(S("o_done"), h + 1)
                        nc.scalar.activation(oT[:, n - 2, :], pb[4 + n % 2][:, 0:T], ACT.Copy)\
                            .then_inc(S("o_out"), 1)

            attention(0, a_oT)
            squares(3)
            root(6, ms[:, 0:T], lny[:, 0:T], rstd[:, 0:T])
            ffn(1)

            def bias_copies():
                for m in range(2):
                    act.wait_ge(S("bias_turned"), m + 1)
                    for half in range(2):
                        src = three(pb[2 * m + half][:, :], 2)
                        dst = biasT[:, 4 * m + 2 * half:4 * m + 2 * half + 2, :]
                        nc.scalar.activation(dst[:, :, 0:P], src[:, :, P:T], ACT.Copy, scale=KV_LORA ** 0.5)\
                            .then_inc(S("bias_cp"), 1)
                        nc.scalar.activation(dst[:, :, P:DIAG], src, ACT.Copy, scale=KV_LORA ** 0.5)\
                            .then_inc(S("bias_cp"), 1)

            def layer(l):
                nn = 7 + 4 * l
                squares(4 + l)
                root(nn, ms[:, 0:T], lny[:, 0:T], rstd[:, 0:T])
                if l == 0:
                    bias_copies()
                for k in range(DC):
                    act.wait_ge(S("xn_done"), 8 * l + k + 1)
                    nc.scalar.activation(xg[:, k, :], xg[:, k, :], ACT.Identity, bias=mod[:, l, k:k + 1])\
                        .then_inc(S("xs_done"), 1)
                product(act, 32 + 16 * l)
                bank = three(pb[0][:, :], 2)
                nc.scalar.activation(b_cq, bank, ACT.Copy).then_inc(S("cq_out"), 1)
                nc.scalar.activation(sq[:, 0:2, :], bank, ACT.Square).then_inc(S("cq_out"), 1)
                product(act, 33 + 16 * l)
                nc.scalar.activation(b_kv, pb[1][:, 0:T], ACT.Copy).then_inc(S("cq_out"), 1)
                nc.scalar.activation(sq[:, 2, :], pb[1][:, 0:T], ACT.Square).then_inc(S("cq_out"), 1)
                nc.scalar.activation(b_kidx, pb[1][:, T:2 * T], ACT.Copy).then_inc(S("cq_out"), 1)
                act.wait_ge(S("widx_done"), l + 1)
                nc.scalar.activation(widx_row[0:8, :], pb[2][0:8, 0:T], ACT.Copy).then_inc(S("cq_out"), 1)
                root(nn + 1, ms[:, :], lny[:, :], rstd[:, :])
                product(act, 35 + 16 * l)
                if l > 0:
                    act.wait_ge(S("glu_done"), 2 * l)
                nc.scalar.activation(b_sg, three(pb[1][:, :], 2), ACT.Sigmoid).then_inc(S("glu_gate"), 1)
                act.wait_ge(S("kv_turned"), l + 1)
                nc.scalar.activation(b_kvt, three(pb[3][:, 0:T], 2), ACT.Copy).then_inc(S("kvt_out"), 1)

                def tap0(i):
                    act.wait_ge(S("glu_done"), 2 * l + i + 1)
                    if l > 0:
                        act.wait_ge(S("yn_done"), l)
                    for c in (2 * i, 2 * i + 1):
                        nc.scalar.activation(b_y[:, c, :], b_a[:, c, 0:T], ACT.Identity,
                                             bias=col("conv_b_2", 4 * l + c),
                                             scale=col("conv_w_2", 124 * l + c)).then_inc(S("conv0_done"), 1)

                tap0(0)
                product(act, 36 + 16 * l)
                for m in range(4):
                    nc.scalar.activation(b_qT[:, 2 * m:2 * m + 2, :], three(pb[4 + m][:, :], 2), ACT.Copy)\
                        .then_inc(S("uq_out"), 1)
                for m in range(2):
                    act.wait_ge(S("qi_proj"), 2 * l + m + 1)
                    nc.scalar.activation(b_qi[:, 2 * m:2 * m + 2, :], three(pb[2 + m][:, :], 2), ACT.Copy)\
                        .then_inc(S("qi_out"), 1)
                for r in range(6):
                    act.wait_ge(S("idx_done"), 6 * l + r + 1)
                    if r >= 2 or l > 0:
                        act.wait_ge(S("relu_read"), 6 * l + r - 1)
                    nc.scalar.activation(relu[r % 2], pb[(4, 5, 6, 7, 2, 3)[r]][:, :], ACT.Relu)\
                        .then_inc(S("relu_done"), 1)
                product(act, 38 + 16 * l)
                act.wait_ge(S("glu_done"), 2 * l + 1)
                nc.scalar.activation(b_sg, three(pb[1][:, :], 2), ACT.Sigmoid).then_inc(S("glu_gate"), 1)
                tap0(1)

                def gate(n):
                    if n % 2 == 0 and n >= 2:
                        m = n // 2 - 1
                        product(act, 39 + 16 * l + m)
                        nc.scalar.activation(y2[:, 2 * m:2 * m + 2, :], three(pb[6 + m % 2][:, :], 2), ACT.Silu)\
                            .then_inc(S("gates_out"), 1)

                attention(1 + l, b_oT, gate)
                act.wait_ge(S("yn_done"), l + 1)
                nc.scalar.activation(sq[:, 0:4, :], b_yn, ACT.Square).then_inc(S("ynsq_done"), 1)
                root(nn + 2, ms[:, 0:T], lny[:, 0:T], rstd[:, 0:T])
                for c in range(CC):
                    act.wait_ge(S("z_done"), CC * l + c + 1)
                    nc.scalar.activation(b_z[:, c, :], b_z[:, c, :], ACT.Silu,
                                         bias=col("conv_ln_b_2", 4 * l + c)).then_inc(S("zs_done"), 1)
                for m in range(4):
                    product(act, 44 + 16 * l + m)
                    bank = three(pb[4 + m][:, :], 2)
                    nc.scalar.activation(b_yT[:, 2 * m:2 * m + 2, :], bank, ACT.Copy).then_inc(S("out_cp"), 1)
                    nc.scalar.activation(sq[:, 2 * m:2 * m + 2, :], bank, ACT.Square).then_inc(S("out_cp"), 1)
                root(nn + 3, ms[:, 0:T], lny[:, 0:T], rstd[:, 0:T])

            for l in range(DEPTH):
                layer(l)
            for m in range(2):
                act.wait_ge(S("h_turned"), 2 * m + 2)
                for half in range(2):
                    nc.scalar.activation(y_rows[:, m, 512 * half:512 * half + 512], pb[2 * m + half][:, :],
                                         ACT.Copy).then_inc(S("y_cp"), 1)

        @block.tensor
        def _(pe):
            mm = nc.tensor.matmul

            def feat(n, bank, x, w=None, nk=DC, chunks=2, at=0, x_ready=None, last_of_slot=True):
                w = slot8(n) if w is None else w
                arrived(pe, n)
                for c in range(chunks):
                    for k in range(nk):
                        if c == 0 and x_ready is not None:
                            x_ready(k)
                        last = mm(bank[:, T * c:T * (c + 1)], w[:, k, at + P * c:at + P * (c + 1)], x[:, k, :],
                                  start=(k == 0), stop=(k == nk - 1))
                return last.then_inc(S("product"), 1) if last_of_slot else last

            def token(n, bank, x, x_ready=None):
                arrived(pe, n)
                for b in range(TB):
                    for k in range(DC):
                        if b == 0 and x_ready is not None:
                            x_ready(k)
                        last = mm(bank[:, T * b:T * (b + 1)], x[:, k, P * b:P * (b + 1)], slot8(n)[:, k, :],
                                  start=(k == 0), stop=(k == DC - 1))
                last.then_inc(S("product"), 1)

            def ss(n, bank, src=None):
                pe.wait_ge(S("sum_done"), n + 1)
                mm(bank, ones[:, 0:P], sq[:, 0, :] if src is None else src, start=True, stop=True)\
                    .then_inc(S("ss_done"), 1)

            def token_rstd(bank):
                for b in range(TB):
                    last = nc.tensor.transpose(bank[:, P * b:P * (b + 1)], rstd[:, P * b:P * (b + 1)], ident)
                last.then_inc(S("rcol_turned"), 1)

            def xg_ready(base):
                return lambda k: pe.wait_ge(S("xg_ready"), base + k + 1)

            pe.wait_ge(S("const_in"), 16)
            pe.wait_ge(S("x_in"), 32)
            for m in range(4):
                for c in range(2):
                    for b in range(TB):
                        last = nc.tensor.transpose(pb[m][:, T * c + P * b:T * c + P * b + P],
                                                   x_rows[:, b, P * (2 * m + c):P * (2 * m + c + 1)], ident)
                last.then_inc(S("x_turned"), 1)
            pe.wait_ge(S("param_in"), 16 * len(PIECES))
            for bank, r0, r1 in ((pb[4], 0, 4), (pb[5], 4, NTURN)):
                for r in range(r0, r1):
                    last = nc.tensor.transpose(bank[:, P * (r - r0):P * (r - r0 + 1)], pstage[:, r, :], ident)
                last.then_inc(S("params_turned"), 1)
            pe.wait_ge(S("rb_in"), 16)
            mm(pb[6][0:8, 0:3 * P], sml[0:BUCKETS, 161:169], pc("bucket", 3 * P)[0:BUCKETS, :],
               start=True, stop=True).then_inc(S("rowsT_done"), 1)

            pe.wait_ge(S("ones_set"), 1)
            feat(0, pb[0], xg, x_ready=xg_ready(0))
            feat(1, pb[1], xg)
            pe.wait_ge(S("cols_done"), 2)
            ss(0, pb[5][:, 0:T])
            feat(2, pb[2], xg)
            feat(3, pb[3], xg)
            pe.wait_ge(S("gw_in"), 32)
            for k in range(DC):
                last = mm(pb[4][0:64, 0:T], m_gw[:, k, :], xg[:, k, :], start=(k == 0), stop=(k == DC - 1))
            last.then_inc(S("m_gate_proj"), 1)
            pe.wait_ge(S("rstd_done"), 1)
            token_rstd(pb[5])
            pe.wait_ge(S("rows_done"), 1)
            token(4, pb[6], xg)
            token(5, pb[7], xg)
            pe.wait_ge(S("m_q_out"), 2)
            token(6, pb[0], xg)
            token(7, pb[1], xg)
            pe.wait_ge(S("m_rows_done"), 1)
            pe.wait_ge(S("rcol_done"), 1)
            for b in range(TB):
                last = nc.tensor.transpose(pb[5][:, 4 * b:4 * b + 4], rows[0:4, 5, P * b:P * (b + 1)],
                                           pc("ident", 4)[0:4, :])
            last.then_inc(S("ccol_turned"), 1)
            head_row = pc("head_row", 4 * P)[0:4, :]

            def spread(h, row, sem):
                last = mm(pb[4 + h // 2][:, T * (h % 2):T * (h % 2 + 1)], head_row[:, P * h:P * (h + 1)], row,
                          start=True, stop=True)
                if h % 2:
                    last.then_inc(S(sem), 1)

            spread(0, rows[0:4, 6, :], "m_spread")
            spread(1, rows[0:4, 6, :], "m_spread")
            pe.wait_ge(S("ccol_done"), 1)
            spread(2, rows[0:4, 6, :], "m_spread")
            spread(3, rows[0:4, 6, :], "m_spread")

            def m_scores(h):
                if h == 0:
                    pe.wait_ge(S("m_k_out"), 2)
                if h >= 2:
                    pe.wait_ge(S("m_p"), h - 1)
                bank = pb[2 + h % 2]
                mm(bank[:, 0:T], m_k[:, h, 0:P], m_q[:, h, :], start=True, stop=True)
                mm(bank[:, T:DIAG], m_k[:, h, P:T], m_q[:, h, P:T], start=True, stop=True)\
                    .then_inc(S("m_scores"), 1)

            def m_square_sum(h):
                pe.wait_ge(S("m_sqs"), h + 1)
                mm(pb[6][0:4, T:2 * T], pc("head_col", 16)[:, 4 * h:4 * h + 4], m_sqn[:, 2 * (h % 2), :],
                   start=False, stop=(h == 3), skip_group_check=True).then_inc(S("m_sums"), 1)

            m_scores(0)
            m_scores(1)
            for h in range(M_HEADS):
                if h == 0:
                    pe.wait_ge(S("m_v_out"), 8)
                if h < 3:
                    if h > 0:
                        pe.wait_ge(S("m_o_scaled"), h)
                    feat(8 + h, pb[7], xg)
                pe.wait_ge(S("m_p"), h + 1)
                pt = m_pt[h % 2]
                sel = pc("head_col", 16)[:, 4 * h:4 * h + 4]
                mm(pb[6][0:4, 0:T], sel, pt[:, 0:T], start=(h == 0), stop=False, skip_group_check=True)
                mm(pb[6][0:4, P:T], sel, pt[:, T:DIAG], start=False, stop=(h == 3), skip_group_check=True)
                if h >= 2:
                    pe.wait_ge(S("m_num_out"), 2 * (h - 1))
                for c in range(2):
                    o = T * c
                    at = M_DV * h + P * c
                    mm(pb[h % 2][:, o:o + T], m_v[:, 0, at:at + P], pt[:, 0:T], start=True, stop=False)
                    last = mm(pb[h % 2][:, o + P:o + T], m_v[:, 1, at:at + P], pt[:, T:DIAG],
                              start=False, stop=True)
                last.then_inc(S("m_num_done"), 1)
                if h < 2:
                    m_scores(h + 2)
                if h >= 1:
                    m_square_sum(h - 1)
            m_square_sum(3)
            pe.wait_ge(S("m_o_scaled"), 3)
            feat(11, pb[7], xg)
            pe.wait_ge(S("rstd_done"), 2)
            for h in range(4):
                spread(h, rows[0:4, 7, :], "f_spread")
            pe.wait_ge(S("m_num_out"), 8)
            for m in range(4):
                feat(12 + m, pb[m], m_y,
                     x_ready=(lambda k: pe.wait_ge(S("m_y_done"), k // 2 + 1)) if m == 0 else None)

            def turn_ada(f, m):
                if m >= 4:
                    pe.wait_ge(S("mod_red"), 6 * f + m - 3)
                for c in range(4):
                    last = nc.tensor.transpose(pb[4 + m % 4][:, P * c:P * (c + 1)],
                                               f_acc[:, P * (4 * m + c):P * (4 * m + c + 1)], ident)
                last.then_inc(S("ada_turned"), 1)

            def ffn(f, nth):
                g0 = FF_STEPS * f

                def up(g, par, turn, x_ready=None):
                    if x_ready is None:
                        pe.wait_ge(S("u_ready"), g - 1)
                    pe.wait_ge(S(f"f_up{par}"), 32 * turn)
                    for j in range(2):
                        w = fring[:, par, j, :].rearrange("p (k n) -> p k n", k=8)
                        for c in range(2):
                            for k in range(DC):
                                if x_ready is not None and j == 0 and c == 0:
                                    x_ready(k)
                                last = mm(pb[4 + 2 * par + j][:, T * c:T * (c + 1)], w[:, k, P * c:P * (c + 1)],
                                          xg[:, k, :], start=(k == 0), stop=(k == DC - 1))
                    last.then_inc(S("up_done"), 1)

                def down(g, par, turn, first=False, end=False):
                    pe.wait_ge(S(f"f_down{par}"), 16 * turn)
                    pe.wait_ge(S("act_ready"), g + 1)
                    w = fring[:, par, 2, :].rearrange("p (k n) -> p k n", k=2)
                    for k in range(2):
                        for m in range(DC):
                            last = mm(pb[m // 2][:, T * (m % 2):T * (m % 2 + 1)], w[:, k, P * m:P * (m + 1)],
                                      f_act[:, par, T * k:T * (k + 1)],
                                      start=(first and k == 0 and m % 2 == 0), stop=(end and k == 1),
                                      skip_group_check=True)
                    last.then_inc(S("down_done"), 1)

                p = g0 % 2
                up(g0, p, g0 // 2 + 1, x_ready=xg_ready(8 + 16 * f))
                ss(nth, pb[0][:, 0:T])
                up(g0 + 1, 1 - p, (g0 + 1) // 2 + 1, x_ready=lambda k: None)
                down(g0, p, g0 // 2 + 1, first=True)
                with pe.Fori(0, 4) as j:
                    for s in range(2):
                        g = 2 * j + (g0 + s + 2)
                        up(g, (g0 + s) % 2, j + ((g0 + s) // 2 + 2))
                        down(g - 1, (g0 + s + 1) % 2, j + ((g0 + s - 1) // 2 + 2))
                g = g0 + FF_STEPS - 1
                up(g, g % 2, g // 2 + 1)
                down(g - 1, (g - 1) % 2, (g - 1) // 2 + 1)
                pe.wait_ge(S("u_ready"), g + 1)
                pe.wait_ge(S("ada_free"), 2 + 16 * (f + 1))
                for m in range(4):
                    turn_ada(f, m)
                down(g, g % 2, g // 2 + 1, end=True)
                for m in (4, 5):
                    turn_ada(f, m)

            ffn(0, 1)

            def attention(a, q, k, v, between=None):
                for n in range(10):
                    if between is not None and n == 0:
                        between(n)
                    if n < 8:
                        h = 8 * a + n
                        if n >= 2:
                            pe.wait_ge(S("max_done"), h - 1)
                        bank = pb[n % 2]
                        mm(bank[:, 0:P], q[:, n, 0:P], k(n)[:, 0:P], start=True, stop=True)
                        mm(bank[:, P:DIAG], q[:, n, P:T], k(n)[:, 0:T], start=True, stop=True)\
                            .then_inc(S("scores_done"), 1)
                    if between is not None and n > 0:
                        between(n)
                    if 1 <= n < 9:
                        h = 8 * a + n - 1
                        pe.wait_ge(S("p_ready"), h + 1)
                        if n >= 3:
                            pe.wait_ge(S("pt_out"), h - 1)
                        bank = pb[2 + (n - 1) % 2]
                        for x in (0, P, 2 * P):
                            last = nc.tensor.transpose(bank[:, x:x + P], p_sb[(n - 1) % 2][:, x:x + P], ident)
                        last.then_inc(S("p_turned"), 1)
                    if n >= 2:
                        h = 8 * a + n - 2
                        pe.wait_ge(S("pt_out"), h + 1)
                        if n >= 4:
                            pe.wait_ge(S("o_out"), h - 1)
                        pt = pt_sb[n % 2]
                        bank = pb[4 + n % 2]
                        mm(bank[:, 0:T], v(0, n - 2), pt[:, 0:T], start=True, stop=False)
                        mm(bank[:, P:T], v(1, n - 2), pt[:, T:DIAG], start=False, stop=True)\
                            .then_inc(S("o_done"), 1)

            token(16, pb[0], xg, x_ready=xg_ready(16))
            pe.wait_ge(S("mod_red"), 4)
            ss(2, pb[7][:, 0:T])
            token(17, pb[1], xg)
            pe.wait_ge(S("mod_red"), 6)
            pe.wait_ge(S("rstd_done"), 4)
            token_rstd(pb[7])
            token(18, pb[2], xg)
            token(19, pb[3], xg)
            token(20, pb[4], a_xq, x_ready=lambda k: pe.wait_ge(S("xq_ready"), k + 1))
            token(21, pb[5], a_xq)
            token(22, pb[6], a_xq)
            for s, bank in ((7, 0), (8, 1), (9, 2), (10, 3), (11, 4)):
                pe.wait_ge(S("tok_out"), 2 * (s - 7 if s < 11 else 4) + 2)
                token(16 + s, pb[bank], a_xq if s == 7 else xg)
            for i, src in ((0, a_kt), (1, a_qt)):
                pe.wait_ge(S("rot_done"), i + 1)
                for m in range(4):
                    if i == 0 and m == 0:
                        pe.wait_ge(S("tok_out"), 16)
                        pe.wait_ge(S("rcol_done"), 2)
                    if i == 1 and m == 0:
                        pe.wait_ge(S("tok_out"), 24)
                    bank = pb[(5, 6, 7, 0, 1, 2, 3, 4)[4 * i + m]]
                    for c in range(2):
                        for b in range(TB):
                            h = 2 * m + c
                            last = nc.tensor.transpose(bank[:, T * c + P * b:T * c + P * (b + 1)],
                                                       src[:, b, P * h:P * (h + 1)], ident)
                    last.then_inc(S("a_turned"), 1)
            pe.wait_ge(S("turn_out"), 8)
            attention(0, a_qT, lambda h: a_kT[:, h, :], lambda b, h: a_v[:, b, A_DH * h:A_DH * (h + 1)])
            for m in range(4):
                if m == 0:
                    pe.wait_ge(S("o_out"), 8)
                feat(28 + m, pb[m], a_oT)

            ffn(1, 3)

            pe.wait_ge(S("skew_in"), 16)
            pe.wait_ge(S("h_ready"), 10)
            skew_f = skew.rearrange("p h t -> p (h t)")
            for m in range(4):
                last = mm(pb[m][:, :], pc("flip", P), skew_f[:, 512 * m:512 * m + 512], start=True, stop=True)
                if m % 2:
                    last.then_inc(S("bias_turned"), 1)
            pe.wait_ge(S("mod_red"), 12)

            def layer(l):
                n = 32 + 16 * l
                nn = 7 + 4 * l
                ns = 4 + 4 * l + l
                ss(ns, pb[7][:, 0:T])
                pe.wait_ge(S("bias_cp"), 8)
                feat(n, pb[0], xg, x_ready=lambda k: pe.wait_ge(S("xs_done"), 8 * l + k + 1))
                feat(n + 1, pb[1], xg)
                pe.wait_ge(S("small_in"), 48 * (l + 1))
                for k in range(DC):
                    last = mm(pb[2][0:8, 0:T], w_widx[:, k, :], xg[:, k, :], start=(k == 0), stop=(k == DC - 1))
                last.then_inc(S("widx_done"), 1)
                ss(ns + 1, pb[3][:, :], src=sq[:, 1:3, :].rearrange("p a b -> p (a b)"))
                pe.wait_ge(S("cq_out"), 6 * l + 6)
                feat(n + 2, pb[0], xg)
                feat(n + 3, pb[1], xg)
                for b in range(TB):
                    last = nc.tensor.transpose(pb[2][:, 8 * b:8 * b + 8], widx_row[0:8, P * b:P * (b + 1)],
                                               pc("ident", 8)[0:8, :])
                last.then_inc(S("wcol_turned"), 1)
                pe.wait_ge(S("cqn_done"), l + 1)
                for b in range(TB):
                    last = nc.tensor.transpose(pb[3][:, P * b:P * (b + 1)], b_kvn[:, P * b:P * (b + 1)], ident)
                last.then_inc(S("kv_turned"), 1)
                arrived(pe, n + 4)
                w_uq = slot(n + 4).rearrange("p (k n) -> p k n", k=2)
                for m in range(4):
                    feat(n + 4, pb[4 + m], b_cqn, w=w_uq, nk=2, at=256 * m, last_of_slot=(m == 3))
                pe.wait_ge(S("wcol_done"), l + 1)
                feat(n + 4, pb[2], b_cqn, w=w_qidx, nk=2, at=0, last_of_slot=False).then_inc(S("qi_proj"), 1)
                pe.wait_ge(S("kvt_out"), l + 1)
                feat(n + 4, pb[3], b_cqn, w=w_qidx, nk=2, at=256, last_of_slot=False)\
                    .then_inc(S("qi_proj"), 1)
                pe.wait_ge(S("uq_out"), 4 * l + 4)
                pe.wait_ge(S("qi_out"), 2 * l + 2)
                for r, heads in enumerate(IDX_ORDER):
                    b = 1 if r < 4 else 0
                    wide = P * (b + 1)
                    for i, h in enumerate(heads):
                        o = 64 * (h % 2)
                        last = mm(pb[(4, 5, 6, 7, 2, 3)[r]][:, wide * i:wide * (i + 1)],
                                  b_qi[o:o + 64, h // 2, P * b:P * (b + 1)], b_kidx[o:o + 64, 0:wide],
                                  start=True, stop=True)
                    last.then_inc(S("idx_done"), 1)
                pe.wait_ge(S("glu_done"), 2 * l + 1)
                feat(n + 5, pb[0], xg)
                feat(n + 6, pb[1], xg)
                pe.wait_ge(S("relu_done"), 6 * l + 6)

                def uv(m):
                    pe.wait_ge(S("o_out"), 8 * (1 + l) + 4 * m + 4)
                    pe.wait_ge(S("max_done"), 8 * (1 + l) + 7 + m)
                    for i in range(2):
                        for half in range(2):
                            h = 4 * m + 2 * i + half
                            last = mm(pb[m][64 * half:64 * half + 64, T * i:T * (i + 1)], w_uv[:, h, :],
                                      b_oT[:, h, :], start=True, stop=True)
                    last.then_inc(S("uv_done"), 1)

                def gates(n_head):
                    if n_head == 8:
                        uv(0)
                    if n_head >= 8:
                        return
                    m, c = n_head // 2, n_head % 2
                    if m >= 2 and c == 0:
                        pe.wait_ge(S("gates_out"), 4 * l + m - 1)
                    last = feat(n + 7 + m, pb[6 + m % 2][:, T * c:T * (c + 1)], xg, chunks=1, at=P * c,
                                last_of_slot=(c == 1))
                    if n_head == 0:
                        pe.wait_ge(S("glu_done"), 2 * l + 2)

                attention(1 + l, b_qT, lambda h: b_kvn, lambda b, h: b_kvt[:, b, :], gates)
                uv(1)
                ss(ns + 2, pb[2][:, 0:T])

                def mix(m, half):
                    w = slot8(n + 12 + m)
                    arrived(pe, n + 12 + m)
                    for c in range(2):
                        for k in range(4 * half, 4 * half + 4):
                            if m == 0 and c == 0 and half == 1 and k % 2 == 0:
                                pe.wait_ge(S("y2_attn"), 2 * l + k // 2 - 1)
                            last = mm(pb[4 + m][:, T * c:T * (c + 1)], w[:, k, P * c:P * (c + 1)], y2[:, k, :],
                                      start=(half == 1 and c == 0 and k == 4), stop=(half == 0 and k == 3),
                                      skip_group_check=True)
                    if half == 0:
                        last.then_inc(S("product"), 1)

                pe.wait_ge(S("o_out"), 8 * (2 + l))
                pe.wait_ge(S("gates_out"), 4 * l + 4)
                mix(0, 1)
                mix(1, 1)
                ss(ns + 3, pb[3][:, 0:T])
                mix(2, 1)
                mix(3, 1)
                w_pw2 = slot(n + 11).rearrange("p (k n) -> p k n", k=CC)
                for m in range(2):
                    feat(n + 11, pb[m], b_z, w=w_pw2, nk=CC, at=256 * m, last_of_slot=(m == 1),
                         x_ready=(lambda k: pe.wait_ge(S("zs_done"), CC * l + k + 1)) if m == 0 else None)
                pe.wait_ge(S("y2_conv"), l + 1)
                for m in range(4):
                    mix(m, 0)
                ss(ns + 4, pb[2][:, 0:T])

            for l in range(DEPTH):
                layer(l)
            pe.wait_ge(S("h_ready"), 14)
            for b in range(TB):
                for half in range(2):
                    for c in range(4):
                        last = nc.tensor.transpose(pb[2 * b + half][:, P * c:P * (c + 1)],
                                                   hT[:, 4 * half + c, P * b:P * (b + 1)], ident)
                    last.then_inc(S("h_turned"), 1)

        @block.vector
        def _(dve):
            v = nc.vector
            done = [0, 0]

            def link(ins):
                ins.then_inc(S("dve_step"), 1)
                done[1] += 1
                return done[0] + done[1]

            def after(n):
                dve.wait_ge(S("dve_step"), n)

            def then(ins):
                after(link(ins))

            def mean_square(n, bank, dst, size):
                dve.wait_ge(S("ss_done"), n + 1)
                return v.tensor_scalar(dst, bank, 1.0 / size, EPS, ALU.mult, ALU.add)

            def newton(nn, a, y, t):
                dve.wait_ge(S("guess_done"), nn + 1)
                then(v.tensor_tensor(t, y, y, ALU.mult))
                then(v.tensor_tensor(t, t, a, ALU.mult))
                then(v.tensor_scalar(t, t, -0.5, 1.5, ALU.mult, ALU.add))
                v.tensor_tensor(y, y, t, ALU.mult).then_inc(S("rstd_done"), 1)
                dve.wait_ge(S("rstd_done"), nn + 1)

            def fold(x, n, last):
                while n > 2:
                    n //= 2
                    then(v.tensor_tensor(x[:, 0:n, :], x[:, 0:n, :], x[:, n:2 * n, :], ALU.add))
                v.tensor_tensor(x[:, 0, :], x[:, 0, :], x[:, 1, :], ALU.add).then_inc(S(last), 1)

            def gained(k, dst, name, sem, at=0):
                for c in range(DC):
                    if c % 4 == 0:
                        dve.wait_ge(S("h_ready"), 2 * k + c // 4 + 1)
                    v.tensor_scalar(dst[:, c, :], hT[:, c, :], col(name, at + c), None, ALU.mult)\
                        .then_inc(S(sem), 1)

            def residual_norm(n, nn):
                dve.wait_ge(S("sq_done"), 2 * (n if n < 4 else 4 + (n - 4) // 5) + 2)
                fold(sq, DC, "sum_done")

            def add_output(bank0=0):
                for m in range(4):
                    x = hT[:, 2 * m:2 * m + 2, :]
                    ins = v.tensor_tensor(x, x, three(pb[bank0 + m][:, :], 2), ALU.add)
                    if m % 2:
                        ins.then_inc(S("h_ready"), 1)

            def add_product(first):
                for m in range(4):
                    product(dve, first + m)
                    x = hT[:, 2 * m:2 * m + 2, :]
                    ins = v.tensor_tensor(x, x, three(pb[m][:, :], 2), ALU.add)
                    if m % 2:
                        ins.then_inc(S("h_ready"), 1)

            dve.wait_ge(S("cols_done"), 2)
            for m in range(4):
                dve.wait_ge(S("x_turned"), m + 1)
                ins = v.tensor_copy(hT[:, 2 * m:2 * m + 2, :], three(pb[m][:, :], 2))
                if m % 2:
                    ins.then_inc(S("h_ready"), 1)
            then(v.tensor_copy(sml[:, 128:129], cols[:, COLS["k_norm"][0]:COLS["k_norm"][0] + 1]))
            then(v.tensor_copy(sml[:, 129:130], cols[:, COLS["b_q_norm"][0]:COLS["b_q_norm"][0] + 1]))
            v.memset(sml[0:ROT, 128:130], 1.0).then_inc(S("ada_free"), 2)
            gained(0, xg, "a_norm", "xg_ready")

            residual_norm(0, 0)
            mean_square(0, pb[5][:, 0:T], ms[:, 0:T], D).then_inc(S("ms_done"), 1)
            dve.wait_ge(S("ms_done"), 1)
            newton(0, ms[:, 0:T], rbc, nwt[:, 0:T])
            for m in range(4):
                product(dve, m)
                dst = (m_q, m_k)[m // 2][:, 2 * (m % 2):2 * (m % 2) + 2, :]
                v.scalar_tensor_tensor(dst, three(pb[m][:, :], 2), M_DQK ** -0.5 if m < 2 else 1.0, rbc2,
                                       ALU.mult, ALU.mult).then_inc(S("m_q_out" if m < 2 else "m_k_out"), 1)
            dve.wait_ge(S("m_gate_proj"), 1)
            dve.wait_ge(S("gb_in"), 32)
            for a in (0, 32):
                r = rows[a:a + 4, 0, :]
                then(v.tensor_tensor(r, pb[4][a:a + 4, 0:T], rstd[a:a + 4, 0:T], ALU.mult))
                then(v.tensor_scalar(r, r, sml[a:a + 4, 160:161], None, ALU.add))
            f = rows[32:36, 0, :]
            v.scalar_tensor_tensor(rows[32:36, 1, :], f, -1.0, f, ALU.mult, ALU.max).then_inc(S("fabs_done"), 1)
            dve.wait_ge(S("rcol_turned"), 1)
            v.tensor_copy(rcol[:, 0:1], pb[5][:, 0:1])
            v.tensor_copy(rcol[:, 1:2], pb[5][:, P:P + 1]).then_inc(S("rcol_done"), 1)
            dve.wait_ge(S("fln_done"), 1)
            lf, B, c, M = rows[0:4, 1, :], rows[0:4, 4, :], rows[0:4, 5, :], rows[0:4, 6, :]
            then(v.scalar_tensor_tensor(lf, f, 0.0, rows[32:36, 3, :], ALU.min, ALU.subtract))
            then(v.tensor_tensor_scan(B, ones[0:4, :], lf, 0.0, ALU.mult, ALU.add))
            then(v.tensor_tensor(c, rows[0:4, 0, :], B, ALU.subtract))
            then(v.tensor_tensor_scan(M, c, c, 0.0, ALU.max, ALU.max))
            then(v.tensor_tensor(rows[0:4, 2, :], B, M, ALU.add))
            v.tensor_scalar(M, M, -1.0, None, ALU.mult).then_inc(S("m_rows_done"), 1)
            dve.wait_ge(S("ccol_turned"), 1)
            v.tensor_copy(sml[:, 0:8], pb[5][:, 0:8]).then_inc(S("ccol_done"), 1)

            def m_decay(h):
                dve.wait_ge(S("m_spread"), h // 2 + 1)
                if h >= 2:
                    dve.wait_ge(S("m_p"), h - 1)
                src = pb[4 + h // 2][:, T * (h % 2):T * (h % 2 + 1)]
                e = m_e[h % 2]
                v.tensor_tensor(e[:, 0:T], src, pc("mask_st", T), ALU.add)
                v.tensor_tensor(e[:, T:DIAG], src[:, P:T], pc("mask_st", P), ALU.add).then_inc(S("m_tmp"), 1)

            def m_output_gate(h):
                product(dve, 8 + h)
                v.tensor_tensor(m_o[:, 2 * h:2 * h + 2, :], three(pb[7][:, :], 2), rbc2, ALU.mult)\
                    .then_inc(S("m_o_scaled"), 1)

            m_decay(0)
            m_decay(1)
            for h in range(M_HEADS):
                dve.wait_ge(S("m_exp"), 2 * h + 2)
                dve.wait_ge(S("m_scores"), h + 1)
                if h >= 2:
                    dve.wait_ge(S("m_num_done"), h - 1)
                v.tensor_tensor(m_pt[h % 2], pb[2 + h % 2][:, 0:DIAG], m_e[h % 2], ALU.mult)\
                    .then_inc(S("m_p"), 1)
                if h < 2:
                    m_decay(h + 2)
                if h < 3:
                    m_output_gate(h)
                dve.wait_ge(S("m_num_out"), 2 * h + 2)
                x = m_sqn[:, 2 * (h % 2):2 * (h % 2) + 2, :]
                v.tensor_tensor(x[:, 0, :], x[:, 0, :], x[:, 1, :], ALU.add).then_inc(S("m_sqs"), 1)
            dve.wait_ge(S("m_sums"), 4)
            dve.wait_ge(S("floor_done"), 1)
            r0, r1 = rows[0:4, 0, :], rows[0:4, 1, :]
            then(v.tensor_copy(r0, pb[6][0:4, 0:T]))
            then(v.scalar_tensor_tensor(r0, r0, -1.0, r0, ALU.mult, ALU.max))
            then(v.tensor_tensor(r0, r0, rows[0:4, 3, :], ALU.max))
            then(v.reciprocal(r1, r0))
            then(v.tensor_tensor(r0, r1, r1, ALU.mult))
            then(v.tensor_tensor(r0, r0, pb[6][0:4, T:2 * T], ALU.mult))
            v.tensor_scalar(rows[0:4, 5, :], r0, 1.0 / M_DV, EPS, ALU.mult, ALU.add).then_inc(S("ms_done"), 1)
            dve.wait_ge(S("guess_done"), 2)
            a, y, t = rows[0:4, 5, :], rows[0:4, 7, :], rows[0:4, 2, :]
            then(v.tensor_tensor(t, y, y, ALU.mult))
            then(v.tensor_tensor(t, t, a, ALU.mult))
            then(v.tensor_scalar(t, t, -0.5, 1.5, ALU.mult, ALU.add))
            then(v.tensor_tensor(t, t, r1, ALU.mult))
            v.tensor_tensor(y, y, t, ALU.mult).then_inc(S("rstd_done"), 1)
            m_output_gate(3)
            for h in range(M_HEADS):
                dve.wait_ge(S("f_spread"), h // 2 + 1)
                dve.wait_ge(S("m_num_out"), 8)
                x = m_num[:, 2 * h:2 * h + 2, :]
                src = pb[4 + h // 2][:, T * (h % 2):T * (h % 2 + 1)].unsqueeze(1).broadcast_to([P, 2, T])
                then(v.tensor_tensor(x, x, src, ALU.mult))
                dve.wait_ge(S("m_o_gate"), h + 1)
                product(dve, 11)
                for i in range(2):
                    c = 2 * h + i
                    ins = v.scalar_tensor_tensor(m_y[:, c, :], m_num[:, c, :], col("a_h_norm", c), m_o[:, c, :],
                                                 ALU.mult, ALU.mult)
                ins.then_inc(S("m_y_done"), 1)
            add_product(12)

            def modulation(l, m0, m1):
                for m in range(m0, m1):
                    dve.wait_ge(S("ada_turned"), 6 * l + m + 1)
                    v.tensor_reduce(mod[:, l, 4 * m:4 * m + 4],
                                    pb[4 + m % 4][:, :].rearrange("p (c k) -> p c k", c=4), AX.X, ALU.add)\
                        .then_inc(S("mod_red"), 1)
                if m1 < 6:
                    return
                dve.wait_ge(S("mod_red"), 6 * l + 6)
                a = COLS["b_ada_2"][0] + 24 * l
                then(v.tensor_tensor(mod[:, l, :], mod[:, l, :], cols[:, a:a + 24], ALU.add))

            def ffn(f, nth, nn):
                gained(2 * f + 1, xg, "f_norm", "xg_ready", at=8 * f)
                residual_norm(nth, nn)
                g0 = FF_STEPS * f
                mean_square(nth, pb[0][:, 0:T], ms[:, 0:T], D).then_inc(S("ms_done"), 1)
                dve.wait_ge(S("ms_done"), nn + 1)
                newton(nn, ms[:, 0:T], rbc, nwt[:, 0:T])

                def step(g, i, par, ada=None):
                    dve.wait_ge(S("up_done"), g + 1)
                    for q in range(2):
                        ins = v.tensor_tensor(f_u[:, q, :, 2:2 + T], three(pb[4 + 2 * par + q][:, :], 2), rbc2,
                                              ALU.mult)
                    ins.then_inc(S("u_ready"), 1)
                    dve.wait_ge(S("u_ready"), g + 1)
                    for tap in (1, 2):
                        marks = [] if tap == 1 else marks
                        new = []
                        for q in (1, 0):
                            for c in range(2):
                                n = 22 * q + 2 * i + c
                                if tap == 1 and c == 0:
                                    dve.wait_ge(S("tap0_done"), 4 * g + 2 * q + 2)
                                if tap == 2:
                                    after(marks[len(new)])
                                ins = v.scalar_tensor_tensor(f_t[q][:, c, :], f_u[:, q, c, tap:tap + T],
                                                             col(f"f_conv_w{f}", 44 * tap + n), f_t[q][:, c, :],
                                                             ALU.mult, ALU.add)
                                if tap == 2 and q == 1 and c == 1:
                                    ins.then_inc(S("gate_conv"), 1)
                                    new.append(None)
                                else:
                                    new.append(link(ins))
                        marks = new
                    if ada is not None:
                        for half in range(2):
                            dve.wait_ge(S(f"ada{half}"), ada + 16 * 8 * f)
                            acc = f_acc[:, 1536 * half:1536 * half + 1536]
                            k = cact[:, bass.ds(i - 2, 1)]
                            ins = v.scalar_tensor_tensor(acc, f_ada[:, half, :], k, acc, ALU.mult, ALU.add)
                            ins.then_inc(S("ada_free"), 1)
                            dve.wait_ge(S("ada_free"), ada_turn(g, half))
                    dve.wait_ge(S("silu_done"), g + 1)
                    after(marks[3])
                    if not isinstance(g, int) or g >= 2:
                        dve.wait_ge(S("down_done"), g - 1)
                    v.tensor_tensor(f_act[:, par, :], f_sg, f_t[0].rearrange("p a b -> p (a b)"), ALU.mult)\
                        .then_inc(S("act_ready"), 1)

                def ada_turn(g, half):
                    return 2 + 16 * f + 2 * (g - g0 - 2) + half + 1

                then(v.memset(f_u[:, :, :, 0:2], 0.0))
                then(v.memset(f_acc, 0.0))
                if f == 0:
                    dve.wait_ge(S("cact_done"), 1)
                for i in (0, 1):
                    step(g0 + i, i, (g0 + i) % 2)
                start = done[1]
                with dve.Fori(0, 4) as j:
                    per = 2 * 7
                    done[0] = per * j
                    for s in range(2):
                        i = 2 * j + s + 2
                        step(g0 + i, i, (g0 + s) % 2, ada=16 * (2 * j + s + 1))
                    assert done[1] - start == per
                done[0], done[1] = 0, start + 4 * per
                i = FF_STEPS - 1
                step(g0 + i, i, (g0 + i) % 2)
                modulation(f, 0, 4)
                dve.wait_ge(S("down_done"), g0 + FF_STEPS)
                add_output()
                modulation(f, 4, 6)

            ffn(0, 1, 2)

            gained(2, xg, "kv_norm", "xg_ready")
            gained(2, a_xq, "b_norm", "xq_ready")
            residual_norm(2, 3)
            mean_square(2, pb[7][:, 0:T], ms[:, 0:T], D).then_inc(S("ms_done"), 1)
            dve.wait_ge(S("ms_done"), 4)
            newton(3, ms[:, 0:T], rbc, nwt[:, 0:T])
            dve.wait_ge(S("rcol_turned"), 2)
            v.tensor_copy(rcol[:, 0:1], pb[7][:, 0:1])
            v.tensor_copy(rcol[:, 1:2], pb[7][:, P:P + 1]).then_inc(S("rcol_done"), 1)
            dve.wait_ge(S("gbc_in"), 32)
            for i, x in ((0, a_kt), (1, a_qt)):
                nn = 4 + i
                dve.wait_ge(S("hsq_done"), i + 1)
                y16 = sml[:, 32:48]
                then(v.tensor_reduce(sml[:, 0:16], a_sq.rearrange("p (h d) -> p h d", d=A_DH), AX.X, ALU.add))
                v.tensor_scalar(sml[:, 0:16], sml[:, 0:16], 1.0 / A_DH, EPS, ALU.mult, ALU.add)\
                    .then_inc(S("ms_done"), 1)
                dve.wait_ge(S("ms_done"), nn + 1)
                newton(nn, sml[:, 0:16], y16, sml[:, 48:64])
                xh = x.rearrange("p b (h d) -> p (b h) d", d=A_DH)
                then(v.tensor_tensor(xh, xh, y16.unsqueeze(2).broadcast_to([P, 16, A_DH]), ALU.mult))
                gain = sml[:, 64 + 32 * i:96 + 32 * i].unsqueeze(1).broadcast_to([P, 16, ROT])
                then(v.tensor_tensor(xh[:, :, 0:ROT], xh[:, :, 0:ROT], gain, ALU.mult))
                x4 = x.rearrange("p b (h d) -> p b h d", d=A_DH)
                cos, sin = [pc(name, TB * HALF).rearrange("p (b d) -> p b d", b=TB) for name in ("cos", "sin")]
                for b in range(TB):
                    x1, x2 = x4[:, b, :, 0:HALF], x4[:, b, :, HALF:ROT]
                    cb = cos[:, b, :].unsqueeze(1).broadcast_to([P, 8, HALF])
                    sb_ = sin[:, b, :].unsqueeze(1).broadcast_to([P, 8, HALF])
                    for r, (u, w) in enumerate(((x1, cb), (x2, sb_), (x2, cb), (x1, sb_))):
                        n = link(v.tensor_tensor(a_rot[r][:, b, :, :], u, w, ALU.mult))
                    after(n)
                    v.tensor_tensor(x1, a_rot[0][:, b, :, :], a_rot[1][:, b, :, :], ALU.subtract)
                    n = v.tensor_tensor(x2, a_rot[2][:, b, :, :], a_rot[3][:, b, :, :], ALU.add)
                    if b == TB - 1:
                        n.then_inc(S("rot_done"), 1)

            def attention(a, scale, added, between=None):
                for n in range(9):
                    if n < 8:
                        h = 8 * a + n
                        dve.wait_ge(S("scores_done"), h + 1)
                        if n >= 2:
                            dve.wait_ge(S("exp_done"), 2 * (h - 1))
                        x, extra, at = sc_sb[n % 2], added(n), 136 + 2 * (n % 2)
                        for b, (lo, hi) in enumerate(((0, P), (P, DIAG))):
                            ins = v.tensor_tensor_reduce(x[:, lo:hi], pb[n % 2][:, lo:hi], extra[:, lo:hi],
                                                         -scale, 3.4e38, ALU.add, ALU.min,
                                                         sml[:, at + b:at + b + 1])
                        ins.then_inc(S("max_done"), 1)
                    if n >= 1:
                        h = 8 * a + n - 1
                        dve.wait_ge(S("exp_done"), 2 * (h + 1))
                        p, at = p_sb[(n - 1) % 2], 140 + 2 * ((n - 1) % 2)
                        then(v.reciprocal(sml[:, at + 4:at + 6], sml[:, at:at + 2]))
                        v.tensor_scalar(p[:, 0:P], p[:, 0:P], sml[:, at + 4:at + 5], None, ALU.mult)
                        v.tensor_scalar(p[:, P:DIAG], p[:, P:DIAG], sml[:, at + 5:at + 6], None, ALU.mult)\
                            .then_inc(S("p_ready"), 1)
                    if between is not None:
                        between(n)

            attention(0, A_DH ** -0.5, lambda n: pc("mask_ts", DIAG))
            add_product(28)
            ffn(1, 3, 6)

            def layer(l):
                n, nn, ns = 32 + 16 * l, 7 + 4 * l, 4 + 5 * l
                gp, gq = sml[:, 148:156], sml[:, 172:180]
                a = COLS["g_pre_2"][0] + 8 * l
                then(v.scalar_tensor_tensor(gp, mod[:, l, 8:16], 1.0, cols[:, a:a + 8], ALU.add, ALU.mult))
                a = COLS["g_post_2"][0] + 8 * l
                then(v.tensor_tensor(gq, mod[:, l, 16:24], cols[:, a:a + 8], ALU.mult))
                residual_norm(ns, nn)
                mean_square(ns, pb[7][:, 0:T], ms[:, 0:T], D).then_inc(S("ms_done"), 1)
                dve.wait_ge(S("ms_done"), nn + 1)
                newton(nn, ms[:, 0:T], rbc, nwt[:, 0:T])
                dve.wait_ge(S("h_ready"), 10 + 2 * l)
                for k in range(DC):
                    v.scalar_tensor_tensor(xg[:, k, :], hT[:, k, :], gp[:, k:k + 1], rbc, ALU.mult, ALU.mult)\
                        .then_inc(S("xn_done"), 1)
                v.memset(b_a[:, :, 0:TAPS - 1], 0.0)
                dve.wait_ge(S("cq_out"), 6 * l + 5)
                v.tensor_tensor(sq[:, 1, :], sq[:, 1, :], sq[:, 0, :], ALU.add).then_inc(S("sum_done"), 1)
                then(mean_square(ns + 1, pb[3][:, 0:T], ms[:, 0:T], 256))
                mean_square(ns + 1, pb[3][:, T:2 * T], ms[:, T:2 * T], 128).then_inc(S("ms_done"), 1)
                dve.wait_ge(S("ms_done"), nn + 2)
                newton(nn + 1, ms[:, :], rstd[:, :], nwt[:, :])
                for c in range(2):
                    v.scalar_tensor_tensor(b_cqn[:, c, :], b_cq[:, c, :], col("q_norm_g_2", 2 * l + c), rbc,
                                           ALU.mult, ALU.mult)
                v.scalar_tensor_tensor(b_kvn, b_kv, col("kv_norm_g_2", l), rstd[:, T:2 * T],
                                       ALU.mult, ALU.mult).then_inc(S("cqn_done"), 1)
                dve.wait_ge(S("wcol_turned"), l + 1)
                v.tensor_scalar(wcol, pb[2][:, 0:16].rearrange("p (a b) -> p a b", a=TB),
                                IDX_HEADS ** -0.5 * D_IDX ** -0.5, None, ALU.mult).then_inc(S("wcol_done"), 1)

                def glu(i):
                    dve.wait_ge(S("glu_gate"), 2 * l + i + 1)
                    product(dve, n + (2, 5)[i])
                    v.tensor_tensor(b_a[:, 2 * i:2 * i + 2, TAPS - 1:TAPS - 1 + T], three(pb[0][:, :], 2), b_sg,
                                    ALU.mult).then_inc(S("glu_done"), 1)

                glu(0)
                marks = [None] * CC

                def taps(i, first, end):
                    for tap in range(first, end):
                        for c in (2 * i, 2 * i + 1):
                            if tap == 1:
                                dve.wait_ge(S("conv0_done"), CC * l + c + 1)
                            else:
                                after(marks[c])
                            marks[c] = link(v.scalar_tensor_tensor(
                                b_y[:, c, :], b_a[:, c, tap:tap + T], col("conv_w_2", 124 * l + 4 * tap + c),
                                b_y[:, c, :], ALU.mult, ALU.add))

                TAPS_FIRST, TAPS_HEAD = 13, 5
                taps(0, 1, 1 + TAPS_FIRST)
                dve.wait_ge(S("wcol_done"), l + 1)
                for r, heads in enumerate(IDX_ORDER):
                    b = 1 if r < 4 else 0
                    wide = P * (b + 1)
                    acc = ts[:, P:DIAG] if b else ts[:, 0:P]
                    dve.wait_ge(S("relu_done"), 6 * l + r + 1)
                    for i, h in enumerate(heads):
                        prev = acc
                        if i > 0:
                            after(last)
                        elif r in (0, 4):
                            prev = pc("mask_top", DIAG)[:, P:DIAG] if b else pc("mask_top", P)
                        else:
                            dve.wait_ge(S("relu_read"), 6 * l + r)
                        ins = v.scalar_tensor_tensor(acc, relu[r % 2][:, wide * i:wide * (i + 1)],
                                                     wcol[:, b, h:h + 1], prev, ALU.mult, ALU.add)
                        if i < len(heads) - 1:
                            last = link(ins)
                        else:
                            ins.then_inc(S("relu_read"), 1)
                dve.wait_ge(S("relu_read"), 6 * l + 6)
                for _ in range(TOPK // 8):
                    m = [link(v.max(best[:, b, :], ts[:, P * b:DIAG if b else P])) for b in range(TB)]
                    for b in range(TB):
                        after(m[b])
                        x = ts[:, P:DIAG] if b else ts[:, 0:P]
                        m[b] = link(v.match_replace(x, best[:, b, :], x, PICKED))
                    after(m[1])
                then(v.tensor_scalar(kmask, ts, -3.2e38, NEG, ALU.is_gt, ALU.mult))
                v.tensor_tensor(kmask, kmask, pc("mask_ts", DIAG), ALU.add).then_inc(S("kmask_done"), 1)

                glu(1)

                def masked(h):
                    dve.wait_ge(S("am_done"), 8 * l + h + 1)
                    return am[h % 2]

                def taps_beside(n_head):
                    left = TAPS - 1 - TAPS_FIRST
                    lo = TAPS_HEAD * n_head
                    hi = lo + TAPS_HEAD
                    if lo < left:
                        taps(0, 1 + TAPS_FIRST + lo, 1 + TAPS_FIRST + min(hi, left))
                    if hi > left:
                        taps(1, 1 + max(lo - left, 0), min(1 + hi - left, TAPS))

                attention(1 + l, KV_LORA ** -0.5, masked, taps_beside)
                taps(1, 1 + 9 * TAPS_HEAD - (TAPS - 1 - TAPS_FIRST), TAPS)
                after(marks[3])
                then(v.tensor_tensor(sq[:, 0:2, :], b_y[:, 0:2, :], b_y[:, 2:4, :], ALU.add))
                v.tensor_tensor(sq[:, 0, :], sq[:, 0, :], sq[:, 1, :], ALU.add).then_inc(S("sum_done"), 1)
                dve.wait_ge(S("gates_out"), 4 * l + 4)
                for m in range(2):
                    dve.wait_ge(S("uv_done"), 2 * l + m + 1)
                    x = y2[:, 4 + 2 * m:6 + 2 * m, :]
                    v.tensor_tensor(x, x, three(pb[m][:, :], 2), ALU.mult).then_inc(S("y2_attn"), 1)
                dve.wait_ge(S("ss_done"), ns + 3)
                mean = pb[2][:, 0:T].unsqueeze(1).broadcast_to([P, CC, T])
                v.scalar_tensor_tensor(b_yn, mean, -1.0 / D_CONV, b_y, ALU.mult, ALU.add)\
                    .then_inc(S("yn_done"), 1)
                dve.wait_ge(S("ynsq_done"), l + 1)
                fold(sq, 4, "sum_done")
                mean_square(ns + 3, pb[3][:, 0:T], ms[:, 0:T], D_CONV).then_inc(S("ms_done"), 1)
                dve.wait_ge(S("ms_done"), nn + 3)
                newton(nn + 2, ms[:, 0:T], rbc, nwt[:, 0:T])
                for c in range(CC):
                    v.scalar_tensor_tensor(b_z[:, c, :], b_yn[:, c, :], col("conv_ln_g_2", 4 * l + c), rbc,
                                           ALU.mult, ALU.mult).then_inc(S("z_done"), 1)
                product(dve, n + 11)
                for m in range(2):
                    x = y2[:, 2 * m:2 * m + 2, :]
                    ins = v.tensor_tensor(x, x, three(pb[m][:, :], 2), ALU.mult)
                ins.then_inc(S("y2_conv"), 1)
                dve.wait_ge(S("out_cp"), 8 * l + 8)
                fold(sq, DC, "sum_done")
                mean_square(ns + 4, pb[2][:, 0:T], ms[:, 0:T], D).then_inc(S("ms_done"), 1)
                dve.wait_ge(S("ms_done"), nn + 4)
                newton(nn + 3, ms[:, 0:T], rbc, nwt[:, 0:T])
                marks = [link(v.scalar_tensor_tensor(b_yT[:, c, :], b_yT[:, c, :], gq[:, c:c + 1], rbc,
                                                     ALU.mult, ALU.mult)) for c in range(DC)]
                for half in range(2):
                    after(marks[4 * half + 3])
                    x = hT[:, 4 * half:4 * half + 4, :]
                    v.tensor_tensor(x, x, b_yT[:, 4 * half:4 * half + 4, :], ALU.add).then_inc(S("h_ready"), 1)

            for l in range(DEPTH):
                layer(l)


INPUTS = ["x", "a_norm", "a_w_in", "a_b_gates", "a_h_norm", "a_w_out", "kv_norm", "w_kv", "k_norm", "b_norm",
          "b_w_q", "b_q_norm", "b_w_o", "f_norm", "f_w_up", "f_conv_w", "f_conv_b", "f_w_down", "c_2",
          "w_ada_2", "b_ada_2", "g_pre_2", "w_in_2", "conv_w_2", "conv_b_2", "conv_ln_g_2", "conv_ln_b_2",
          "w_pw2_2", "q_norm_g_2", "w_uq_2", "w_qidx_2", "kv_norm_g_2", "w_uv_2", "rel_bias_2", "w_out_2",
          "g_post_2"]


def kernel(**inputs):
    import concourse.bacc as bacc
    from concourse.bass_utils import run_bass_kernel_spmd

    nc = bacc.Bacc("TRN2", target_bir_lowering=False, num_devices=1)
    arrays, handles = {}, {}
    for name in INPUTS:
        a = np.ascontiguousarray(inputs[name])
        arrays[f"in_{name}"] = a
        handles[name] = nc.dram_tensor(f"in_{name}", a.shape, mybir.dt.from_np(a.dtype), kind="ExternalInput").ap()
    a = shape_constants()
    arrays["in_consts"] = a
    handles["consts"] = nc.dram_tensor("in_consts", a.shape, F32, kind="ExternalInput").ap()
    out = nc.dram_tensor("out", (1, T, D), F32, kind="ExternalOutput").ap()
    model(nc, handles, out)
    return run_bass_kernel_spmd(nc, [arrays], core_ids=[0]).results[0]["out"]
```

```python
from contextlib import ExitStack

import numpy as np

import concourse.bass as bass
from concourse import mybir

F32 = mybir.dt.float32
ALU = mybir.AluOpType
ACT = mybir.ActivationFunctionType
AX = mybir.AxisListType

P = 128
T = 256
TB = T // P
D = 1024
DC = D // P
EPS = 1e-6
M_HEADS, M_DQK, M_DV = 4, 128, 256
A_DH = 128
ROT = A_DH // 4
HALF = ROT // 2
D_FF = 2816
FF_STEPS = D_FF // 256
DEPTH = 2
D_CONV, TAPS = 512, 31
CC = D_CONV // P
IDX_HEADS, D_IDX = 8, 64
KV_LORA = 128
TOPK = 64
IDX_ORDER = ((0, 2), (1, 3), (4, 6), (5, 7), (0, 2, 4, 6), (1, 3, 5, 7))
BUCKETS, MAX_DISTANCE = 32, 128
NEG = -1e30
CAUSAL = -3.0e38
PICKED = -3.4e38
RING = 8
DIAG = P + T

COLS = {}
_n = 0
for _name, _rows in ([("f_conv_w0", 132), ("f_conv_b0", 44), ("f_conv_w1", 132), ("f_conv_b1", 44),
                      ("a_norm", 8), ("f_norm", 16), ("kv_norm", 8), ("b_norm", 8), ("a_h_norm", 8),
                      ("k_norm", 1), ("b_q_norm", 1), ("c_2", 8), ("b_ada_2", 48), ("g_pre_2", 16),
                      ("conv_w_2", 248), ("conv_b_2", 8), ("conv_ln_g_2", 8), ("conv_ln_b_2", 8),
                      ("q_norm_g_2", 4), ("kv_norm_g_2", 2), ("g_post_2", 16)]):
    COLS[_name] = (_n, _rows)
    _n += _rows
NCOL = -(-_n // P) * P
PIECES = []
for _name, (_at, _rows) in COLS.items():
    _done = 0
    while _done < _rows:
        _m = min(_rows - _done, P - (_at + _done) % P)
        PIECES.append((_name, _done, _at + _done, _m))
        _done += _m
NTURN = NCOL // P

CONST = {}
_n = 0
for _name, _w in (("ident", P), ("flip", P), ("mask_st", T), ("mask_ts", DIAG), ("mask_top", DIAG),
                  ("cos", TB * HALF), ("sin", TB * HALF), ("head_col", 16), ("head_row", 4 * P),
                  ("bucket", 3 * P)):
    CONST[_name] = (_n, _w)
    _n += _w
NCONST = _n


def shape_constants():
    c = np.zeros((P, NCONST), np.float32)

    def put(name, a):
        c[:a.shape[0], CONST[name][0]:CONST[name][0] + a.shape[1]] = a

    p = np.arange(P)
    put("ident", np.eye(P, dtype=np.float32))
    put("flip", np.eye(P, dtype=np.float32)[::-1])
    later = np.where(p[None, :] < p[:, None], NEG, 0.0)
    put("mask_st", np.concatenate([later, np.zeros((P, P))], 1))
    ahead = p[None, :] > p[:, None]
    for name, v in (("mask_ts", NEG), ("mask_top", CAUSAL)):
        m = np.where(ahead, v, 0.0)
        put(name, np.concatenate([m, np.zeros((P, P)), m], 1))
    inv = np.float32(500000.0) ** (-np.arange(0, ROT, 2, dtype=np.float32) / np.float32(ROT))
    ang = np.arange(T, dtype=np.float32)[:, None] * inv.astype(np.float32)[None, :]
    for name, f in (("cos", np.cos), ("sin", np.sin)):
        t = f(ang).astype(np.float32).reshape(TB, P, HALF)
        put(name, t.transpose(1, 0, 2).reshape(P, TB * HALF))
    hc = np.zeros((P, 4, 4))
    hr = np.zeros((4, 4, P))
    for h in range(4):
        hc[:, h, h] = 1
        hr[h, h, :] = 1
    put("head_col", hc.reshape(P, 16))
    put("head_row", hr.reshape(4, 4 * P))
    dist = np.maximum(T - 1 - np.arange(3 * P), 0)
    exact = BUCKETS // 2
    near = np.maximum(dist, 1).astype(np.float32)
    large = exact + (np.log(near / np.float32(exact)) / np.float32(np.log(MAX_DISTANCE / exact))
                     * np.float32(BUCKETS - exact)).astype(np.int32)
    bucket = np.where(dist < exact, dist, np.minimum(large, BUCKETS - 1))
    put("bucket", (np.arange(BUCKETS)[:, None] == bucket[None, :]).astype(np.float32))
    return c


def model(nc, I, out):
    with ExitStack() as ctx:
        def sb(name, shape):
            return ctx.enter_context(nc.sbuf_tensor(name, shape, F32))

        sems = {}

        def S(name):
            if name not in sems:
                sems[name] = ctx.enter_context(nc.semaphore(name))
            return sems[name]

        ring = sb("ring", [P, RING, 2048])
        fring = sb("fring", [P, 2, 3, 2048])
        work = sb("work", [P, 6 * 2048])
        hT = sb("hT", [P, DC, T])
        xg = sb("xg", [P, DC, T])
        sq = sb("sq", [P, DC, T])
        consts = sb("consts", [P, NCONST])
        cols = sb("cols", [P, NCOL])
        ones = sb("ones", [P, T])
        ms = sb("ms", [P, 2 * T])
        lny = sb("lny", [P, 2 * T])
        nwt = sb("nwt", [P, 2 * T])
        rstd = sb("rstd", [P, 2 * T])
        rcol = sb("rcol", [P, TB])
        sml = sb("sml", [P, 192])
        mod = sb("mod", [P, DEPTH, 24])
        cact = sb("cact", [P, 8])
        pb = [ctx.enter_context(nc.psum_tensor(f"bank{i}", [P, 512], F32)) for i in range(8)]

        def W(a, b):
            return work[:, a:b]

        def pc(name, w, at=0):
            a = CONST[name][0] + at
            return consts[:, a:a + w]

        def col(name, i):
            return cols[:, bass.ds(COLS[name][0] + i, 1)]

        def three(ap, n):
            return ap.rearrange("p (a b) -> p a b", a=n)

        ident = pc("ident", P)
        rbc = rstd[:, 0:T]
        rbc2 = rbc.unsqueeze(1).broadcast_to([P, 2, T])

        m_q, m_k = three(W(0, 1024), 4), three(W(1024, 2048), 4)
        m_v = three(W(2048, 4096), TB)
        m_o = three(W(4096, 6144), DC)
        m_num = three(W(6144, 8192), DC)
        m_gw = W(8192, 8704).rearrange("p (k n) -> p k n", k=DC)
        m_e = [W(8704 + 384 * i, 9088 + 384 * i) for i in range(2)]
        m_pt = [W(9472 + 384 * i, 9856 + 384 * i) for i in range(2)]
        m_y = xg
        m_sqn = sq[:, 0:4, :]
        rows = W(9856, 11904)[0:36, :].rearrange("p (a t) -> p a t", a=8)
        scratch = nc.dram_tensor("bias_rows", (8, 3 * P), F32)
        pstage = three(W(0, NCOL), NTURN)
        a_norm_rows = W(11776, 11904)[0:8, :]
        a_norm_cols = sml[:, 181:189]
        a_xq = three(W(0, 2048), DC)
        a_qT = three(W(0, 2048), 8)
        a_kt, a_qt = three(W(2048, 4096), TB), three(W(4096, 6144), TB)
        a_v = three(W(6144, 8192), TB)
        a_kT = three(W(8192, 10240), 8)
        a_oT = three(W(10240, 12288), 8)
        a_sq = W(10240, 12288)
        a_rot = [W(10240 + 256 * i, 10496 + 256 * i).rearrange("p (b h d) -> p b h d", b=TB, h=8)
                 for i in range(4)]
        f_ada = three(W(0, 3072), 2)
        f_acc = W(3072, 6144)
        f_act = three(W(6144, 7168), 2)
        f_t = [three(W(7168 + 512 * i, 7680 + 512 * i), 2) for i in range(2)]
        f_u = W(8192, 8192 + 4 * 258).rearrange("p (g c t) -> p g c t", g=2, c=2)
        f_sg = W(9300, 9812)
        sqf = sq[:, :, :].rearrange("p a b -> p (a b)")
        sc_sb = [sqf[:, DIAG * i:DIAG * (i + 1)] for i in range(2)]
        p_sb = [sqf[:, DIAG * (2 + i):DIAG * (3 + i)] for i in range(2)]
        pt_sb = [sqf[:, DIAG * 4:DIAG * 5], nwt[:, 0:DIAG]]
        x_rows = three(sqf, TB)
        y_rows = x_rows
        fr = fring[:, :, :, :].rearrange("p a b c -> p (a b c)")
        biasT = fr[:, 0:3072].rearrange("p (h t) -> p h t", h=8)
        skew = fr[:, 3072:5120].rearrange("p (h t) -> p h t", h=8)
        y2 = three(fr[:, 5120:7168], DC)
        small_w = fr[:, 7168:7168 + 1088 + 512]
        w_qidx = small_w[:, 64:1088].rearrange("p (k n) -> p k n", k=2)
        w_uv = small_w[:, 1088:1600].rearrange("p (h n) -> p h n", h=8)
        am = [fr[:, 8768 + DIAG * i:8768 + DIAG * (i + 1)] for i in range(2)]
        kmask = fr[:, 9536:9536 + DIAG]
        ts = fr[:, 9920:9920 + DIAG]
        relu = [fr[:, 10304 + 512 * i:10816 + 512 * i] for i in range(2)]
        wcol = fr[:, 11328:11344].rearrange("p (a b) -> p a b", a=TB)
        best = fr[:, 11344:11360].rearrange("p (a b) -> p a b", a=TB)
        widx_row = fr[:, 11360:11616]
        b_cq = three(W(0, 512), 2)
        b_kv = W(512, 768)
        b_kidx = W(768, 1024)
        b_cqn = three(W(1024, 1536), 2)
        b_kvn = W(1536, 1792)
        b_kvt = three(W(1792, 2048), TB)
        b_qT = three(W(2048, 4096), 8)
        b_qi = three(W(4096, 5120), 4)
        b_yn = three(W(5120, 6144), CC)
        b_a = W(6144, 6144 + CC * (T + TAPS - 1)).rearrange("p (c t) -> p c t", c=CC)
        b_y = three(W(7300, 8324), CC)
        b_z = three(W(8324, 9348), CC)
        b_sg = three(W(9348, 9860), 2)
        b_oT = three(W(10240, 12288), 8)
        b_ytok = W(2048, 4096).rearrange("p (b n) -> p b n", b=TB)
        diag = three(ms[:, 0:T], TB)

        def cut(w, c, n=256):
            return w.rearrange("(k p) n -> p k n", p=P)[:, :, c:c + n]

        def slot(n):
            return ring[:, n % RING, :]

        def slot8(n):
            return slot(n).rearrange("p (k n) -> p k n", k=8)

        loads = [[(slot8(n), cut(I["a_w_in"][0], 256 * n))] for n in range(12)]
        loads += [[(slot8(n), cut(I["a_w_out"][0], 256 * (n - 12)))] for n in range(12, 16)]
        loads += [[(slot8(n), cut(I["w_kv"], 256 * (n - 16)))] for n in range(16, 20)]
        loads += [[(slot8(n), cut(I["b_w_q"][0], 256 * (n - 20)))] for n in range(20, 24)]
        loads += [[(slot8(n), cut(I["w_kv"], D + 256 * (n - 24)))] for n in range(24, 28)]
        loads += [[(slot8(n), cut(I["b_w_o"][0], 256 * (n - 28)))] for n in range(28, 32)]
        O_VAL, O_GATE, O_GC, O_CQ, O_KV, O_GA = 0, 512, 1024, 1536, 1792, 1992
        for l in range(DEPTH):
            n = 32 + 16 * l
            w = I["w_in_2"][l]
            loads.append([(slot8(n), cut(w, O_CQ))])
            s = slot8(n + 1)
            loads.append([(s[:, :, 0:200], cut(w, O_KV, 200))])
            for i, c in ((2, O_VAL), (3, O_GATE)):
                loads.append([(slot8(n + i), cut(w, c))])
            loads.append([(slot(n + 4).rearrange("p (k n) -> p k n", k=2),
                           I["w_uq_2"][l].rearrange("(k p) n -> p k n", p=P))])
            for i, c in enumerate((O_VAL + 256, O_GATE + 256, O_GC, O_GC + 256, O_GA, O_GA + 256)):
                loads.append([(slot8(n + 5 + i), cut(w, c))])
            loads.append([(slot(n + 11).rearrange("p (k n) -> p k n", k=CC),
                           I["w_pw2_2"][l].rearrange("(k p) n -> p k n", p=P))])
            loads += [[(slot8(n + 12 + i), cut(I["w_out_2"][l], 256 * i))] for i in range(4)]
        landed = [0] * RING
        ring_count = []
        for n, parts in enumerate(loads):
            landed[n % RING] += 16 * len(parts)
            ring_count.append(landed[n % RING])

        def arrived(eng, n):
            eng.wait_ge(S(f"ring{n % RING}"), ring_count[n])

        def product(eng, n):
            eng.wait_ge(S("product"), n + 1)

        def lns(n):
            return n + 1 - (n - 4 + 2) // 4 if n >= 4 else n + 1

        block = ctx.enter_context(nc.Block())

        @block.sync
        def _(sp):
            def load(n):
                if n >= RING:
                    product(sp, n - RING)
                for dst, src in loads[n]:
                    sp.dma_start(dst, src).then_inc(S(f"ring{n % RING}"), 16)

            def load_ffn(f, i, par, first):
                up = I["f_w_up"][f].rearrange("(k p) n -> p k n", p=P)
                down = I["f_w_down"][f].rearrange("(k p) n -> p k n", p=P)
                g = FF_STEPS * f + i
                if not first:
                    sp.wait_ge(S("up_done"), g - 1)
                for j, c in enumerate((i * 256, D_FF + i * 256)):
                    sp.dma_start(fring[:, par, j, :].rearrange("p (k n) -> p k n", k=8),
                                 up[:, :, bass.ds(c, 256)]).then_inc(S(f"f_up{par}"), 16)
                if not first:
                    sp.wait_ge(S("down_done"), g - 1)
                sp.dma_start(fring[:, par, 2, :].rearrange("p (k n) -> p k n", k=2),
                             down[:, bass.ds(2 * i, 2), :]).then_inc(S(f"f_down{par}"), 16)

            def load_ada(l, k):
                src = I["w_ada_2"][l].rearrange("(k p) n -> p k n", p=P)
                for half in range(2):
                    sp.wait_ge(S("ada_free"), 2 * (8 * l + k) + half + 1)
                    sp.dma_start(f_ada[:, half, :].unsqueeze(1),
                                 src[:, bass.ds(k, 1), 1536 * half:1536 * half + 1536])\
                        .then_inc(S(f"ada{half}"), 16)

            def ffn_loads(f):
                sp.wait_ge(S("up_done"), FF_STEPS * f + 1)
                with sp.Fori(0, 4) as j:
                    for s in range(2):
                        load_ffn(f, 2 * j + s + 2, (FF_STEPS * f + s) % 2, False)
                        load_ada(f, 2 * j + s)
                load_ffn(f, FF_STEPS - 1, (FF_STEPS * f + FF_STEPS - 1) % 2, False)

            sp.wait_ge(S("x_in"), 32)
            for n in range(RING):
                if n == 2:
                    sp.wait_ge(S("param_in"), 16 * len(PIECES))
                load(n)
            load_ffn(0, 0, 0, True)
            load_ffn(0, 1, 1, True)
            for n in range(8, 24):
                load(n)
            ffn_loads(0)
            load_ffn(1, 0, 1, False)
            load_ffn(1, 1, 0, False)
            for n in range(24, 40):
                load(n)
            ffn_loads(1)
            sp.wait_ge(S("down_done"), 2 * FF_STEPS - 1)
            sp.wait_ge(S("rows_out"), 16)
            sp.dma_start(skew, bass.AP(scratch, 0, [[1, P], [3 * P, 8], [1, T]])).then_inc(S("skew_in"), 16)
            sp.wait_ge(S("down_done"), 2 * FF_STEPS)
            for l in range(DEPTH):
                if l > 0:
                    sp.wait_ge(S("uv_done"), 2 * l)
                sp.dma_start(w_qidx, I["w_qidx_2"][l].rearrange("(k p) n -> p k n", p=P))\
                    .then_inc(S("small_in"), 16)
                sp.dma_start(w_uv, I["w_uv_2"][l].rearrange("h p n -> p h n")).then_inc(S("small_in"), 16)
                for n in (range(40, 48) if l == 0 else range(48, 64)):
                    load(n)
            for half in range(2):
                for b in range(TB):
                    sp.wait_ge(S("y_cp"), 2 * half + b + 1)
                    sp.dma_start(out[0, P * b:P * (b + 1), 512 * half:512 * half + 512],
                                 y_rows[:, b, 512 * half:512 * half + 512]).then_inc(S("stored"), 16)
            sp.wait_ge(S("stored"), 64)

        @block.gpsimd
        def _(pool):
            nc.gpsimd.memset(ones[:, :], 1.0).then_inc(S("ones_set"), 1)
            nc.gpsimd.memset(sml[:, 180:181], EPS).then_inc(S("ones_set"), 1)
            nc.gpsimd.memset(m_gw[:, :, :], 0.0).then_inc(S("gw_zero"), 1)
            for l in range(DEPTH):
                for h in range(8):
                    n = 8 * l + h
                    pool.wait_ge(S("kmask_done"), l + 1)
                    if h == 0:
                        pool.wait_ge(S("bias_cp"), 8)
                    if n >= 2:
                        pool.wait_ge(S("max_done"), 8 + n - 1)
                    nc.gpsimd.tensor_tensor(am[h % 2], biasT[:, h, :], kmask, ALU.add)\
                        .then_inc(S("am_done"), 1)

        @block.scalar
        def _(act):
            done = [0]

            def link(ins):
                done[0] = done[0] + 1
                ins.then_inc(S("act_step"), 1)
                return done[0]

            def after(n):
                act.wait_ge(S("act_step"), n)

            def tables(name):
                act.preload_act_table_set(name)

            LN_EXP, SIGMOID, SILU = "natural_log_exp_and_others", "sigmoid_and_others", "silu_and_others"

            def guess(nn, tmp, dst):
                if nn >= 1:
                    act.wait_ge(S("rstd_done"), nn)
                nc.scalar.activation(dst, tmp, ACT.Exp, scale=-0.5).then_inc(S("guess_done"), 1)

            roots_of_ms = [0]

            def root_of_ms(nn, src, tmp, dst):
                roots_of_ms[0] += 1
                act.wait_ge(S("ms_done"), roots_of_ms[0])
                if nn >= 1:
                    act.wait_ge(S("rstd_done"), nn)
                after(link(nc.scalar.activation(tmp, src, ACT.Ln)))
                guess(nn, tmp, dst)

            def root(nn, n, bank, size):
                act.wait_ge(S("ss_done"), n + 1)
                if nn >= 1:
                    act.wait_ge(S("rstd_done"), nn)
                nc.scalar.activation(lny[:, 0:T], bank, ACT.Ln, scale=1.0 / size, bias=sml[:, 180:181])\
                    .then_inc(S("ln_done"), 1)
                act.wait_ge(S("ln_done"), lns(n))
                guess(nn, lny[:, 0:T], rstd[:, 0:T])

            def squares(k):
                tables(LN_EXP)
                for m in range(4):
                    act.wait_ge(S("h_ready"), 4 * k + m + 1)
                    nc.scalar.activation(sq[:, 2 * m:2 * m + 2, :], hT[:, 2 * m:2 * m + 2, :],
                                         ACT.Square).then_inc(S("sq_done"), 1)

            act.dma_start(ident, I["consts"][:, 0:P]).then_inc(S("ident_in"), 16)
            act.dma_start(a_norm_rows, I["a_norm"].rearrange("l (c p) -> (l c) p", p=P)).then_inc(S("a_in"), 16)
            act.dma_start(x_rows[:, 0, :], I["x"][0, 0:P, :]).then_inc(S("x_in"), 16)
            act.dma_start(x_rows[:, 1, :], I["x"][0, P:T, :]).then_inc(S("x_in"), 16)
            flat = {"f_conv_w0": I["f_conv_w"][0].rearrange("j (c p) -> j c p", p=P),
                    "f_conv_w1": I["f_conv_w"][1].rearrange("j (c p) -> j c p", p=P),
                    "f_conv_b0": I["f_conv_b"][0].rearrange("(c p) -> c p", p=P),
                    "f_conv_b1": I["f_conv_b"][1].rearrange("(c p) -> c p", p=P)}
            for name, first, r, m in PIECES:
                src = I[name] if name in I else flat[name]
                if name in ("kv_norm", "k_norm"):
                    src = src.rearrange("(c p) -> c p", p=P)
                elif name == "conv_w_2":
                    src = src.rearrange("l j (c p) -> (l j c) p", p=P)
                elif name in I:
                    src = src.rearrange("l (c p) -> (l c) p", p=P)
                elif "conv_w" in name:
                    src = src.rearrange("j c p -> (j c) p")
                act.dma_start(pstage[r % P:r % P + m, r // P, :], src[first:first + m, :])\
                    .then_inc(S("param_in"), 16)
            act.dma_start(consts[:, P:NCONST], I["consts"][:, P:NCONST]).then_inc(S("const_in"), 16)
            act.wait_ge(S("gw_zero"), 1)
            w = I["a_w_in"][0].rearrange("(k p) n -> p k n", p=P)
            act.dma_start(m_gw[:, :, 0:4], w[:, :, 3072:3076]).then_inc(S("gw_in"), 16)
            act.dma_start(m_gw[:, :, 32:36], w[:, :, 3076:3080]).then_inc(S("gw_in"), 16)
            act.dma_start(sml[0:4, 160:161], I["a_b_gates"][0, 0, :].unsqueeze(1)).then_inc(S("gb_in"), 16)
            act.dma_start(sml[32:36, 160:161], I["a_b_gates"][0, 1, :].unsqueeze(1)).then_inc(S("gb_in"), 16)
            act.dma_start(sml[0:BUCKETS, 161:169], I["rel_bias_2"]).then_inc(S("rb_in"), 16)
            act.dma_start(sml[:, 64:96], I["k_norm"][0:ROT].partition_broadcast(P)).then_inc(S("gbc_in"), 16)
            act.dma_start(sml[:, 96:128], I["b_q_norm"][0, 0:ROT].partition_broadcast(P)).then_inc(S("gbc_in"), 16)

            act.wait_ge(S("x_turned"), 4)
            squares(0)
            act.wait_ge(S("params_turned"), 2)
            nc.scalar.activation(cols[:, 0:512], pb[4][:, :], ACT.Copy).then_inc(S("cols_done"), 1)
            nc.scalar.activation(cols[:, 512:NCOL], pb[5][:, 0:NCOL - 512], ACT.Copy)\
                .then_inc(S("cols_done"), 1)
            root(0, 0, pb[5][:, 0:T], D)
            act.wait_ge(S("rowsT_done"), 1)
            nc.scalar.activation(work[0:8, 11904:12288], pb[6][0:8, 0:3 * P], ACT.Copy)\
                .then_inc(S("rows_done"), 1)
            act.wait_ge(S("rows_done"), 1)
            act.dma_start(scratch.ap(), work[0:8, 11904:12288]).then_inc(S("rows_out"), 16)
            act.wait_ge(S("fabs_done"), 1)
            after(link(nc.scalar.activation(rows[32:36, 2, :], rows[32:36, 1, :], ACT.Exp, scale=-1.0)))
            nc.scalar.activation(rows[32:36, 3, :], rows[32:36, 2, :], ACT.Ln, bias=1.0)\
                .then_inc(S("fln_done"), 1)
            for s in range(4):
                product(act, 4 + s)
                if s == 0:
                    act.wait_ge(S("rcol_done"), 1)
                for b in range(TB):
                    nc.scalar.activation(m_v[:, b, 256 * s:256 * s + 256], pb[(6 + s) % 8][:, 256 * b:256 * b + 256],
                                         ACT.Copy, scale=rcol[:, b:b + 1]).then_inc(S("m_v_out"), 1)
            act.wait_ge(S("m_rows_done"), 1)
            nc.scalar.activation(rows[0:4, 3, :], rows[0:4, 2, :], ACT.Exp, scale=-1.0)\
                .then_inc(S("floor_done"), 1)

            def decay(h):
                act.wait_ge(S("m_tmp"), h + 1)
                if h == 0:
                    act.wait_ge(S("ccol_done"), 1)
                e = m_e[h % 2]
                nc.scalar.activation(e[:, 0:T], e[:, 0:T], ACT.Exp, bias=sml[:, h:h + 1])\
                    .then_inc(S("m_exp"), 1)
                nc.scalar.activation(e[:, T:DIAG], e[:, T:DIAG], ACT.Exp, bias=sml[:, 4 + h:5 + h])\
                    .then_inc(S("m_exp"), 1)

            def numer(h):
                act.wait_ge(S("m_num_done"), h + 1)
                bank = pb[h % 2][:, :].rearrange("p (a b) -> p a b", a=2)
                nc.scalar.activation(m_num[:, 2 * h:2 * h + 2, :], bank, ACT.Copy).then_inc(S("m_num_out"), 1)
                if h >= 2:
                    act.wait_ge(S("m_sqs"), h - 1)
                nc.scalar.activation(m_sqn[:, 2 * (h % 2):2 * (h % 2) + 2, :], bank, ACT.Square)\
                    .then_inc(S("m_num_out"), 1)

            decay(0)
            for h in range(4):
                if h < 3:
                    decay(h + 1)
                numer(h)
            root_of_ms(1, rows[0:4, 5, :], rows[0:4, 6, :], rows[0:4, 7, :])
            tables(SIGMOID)
            for h in range(4):
                act.wait_ge(S("m_o_scaled"), h + 1)
                nc.scalar.activation(m_o[:, 2 * h:2 * h + 2, :], m_o[:, 2 * h:2 * h + 2, :], ACT.Sigmoid)\
                    .then_inc(S("m_o_gate"), 1)

            def ffn(f):
                def step(g, i, par):
                    act.wait_ge(S("u_ready"), g + 1)
                    act.wait_ge(S("act_ready"), g)
                    for v in range(2):
                        for c in range(2):
                            n = 22 * v + 2 * i + c
                            nc.scalar.activation(f_t[v][:, c, :], f_u[:, v, c, 0:T], ACT.Identity,
                                                 bias=col(f"f_conv_b{f}", n),
                                                 scale=col(f"f_conv_w{f}", n)).then_inc(S("tap0_done"), 1)
                    act.wait_ge(S("gate_conv"), g + 1)
                    nc.scalar.activation(f_sg.rearrange("p (a b) -> p a b", a=2), f_t[1], ACT.Silu)\
                        .then_inc(S("silu_done"), 1)

                g0 = FF_STEPS * f
                for i in (0, 1):
                    step(g0 + i, i, (g0 + i) % 2)
                with act.Fori(0, 4) as j:
                    for s in range(2):
                        i = 2 * j + s + 2
                        step(g0 + i, i, (g0 + s) % 2)
                step(g0 + FF_STEPS - 1, FF_STEPS - 1, (g0 + FF_STEPS - 1) % 2)

            squares(1)
            root(2, 1, pb[0][:, 0:T], D)
            tables(SILU)
            nc.scalar.activation(cact[:, :], cols[:, COLS["c_2"][0]:COLS["c_2"][0] + 8], ACT.Silu)\
                .then_inc(S("cact_done"), 1)
            ffn(0)

            squares(2)
            root(3, 2, pb[7][:, 0:T], D)
            banks = [0, 1, 2, 3, 4, 5, 6, 0, 1, 2, 6, 7]

            def rows_out(s):
                product(act, 16 + s)
                dst = (a_kt, a_qt, a_v)[s // 4]
                for b in range(TB):
                    c = 256 * (s % 4)
                    nc.scalar.activation(dst[:, b, c:c + 256], pb[banks[s]][:, 256 * b:256 * b + 256],
                                         ACT.Copy, scale=rcol[:, b:b + 1]).then_inc(S("tok_out"), 1)

            def head_squares(i):
                act.wait_ge(S("tok_out"), 8 * (i + 1))
                if i == 0:
                    act.wait_ge(S("rows_out"), 16)
                if i == 1:
                    act.wait_ge(S("rot_done"), 1)
                src = (a_kt, a_qt)[i]
                nc.scalar.activation(a_sq, src.rearrange("p a b -> p (a b)"), ACT.Square)\
                    .then_inc(S("hsq_done"), 1)
                root_of_ms(4 + i, sml[:, 0:16], sml[:, 16:32], sml[:, 32:48])

            act.wait_ge(S("rcol_done"), 2)
            for s in range(4):
                rows_out(s)
            head_squares(0)
            for s in range(4, 8):
                rows_out(s)
            head_squares(1)
            for s in (8, 9):
                rows_out(s)
            for i, dst in ((0, a_kT), (1, a_qT)):
                for m in range(4):
                    act.wait_ge(S("a_turned"), 4 * i + m + 1)
                    nc.scalar.activation(dst[:, 2 * m:2 * m + 2, :],
                                         three(pb[(5, 6, 7, 0, 1, 2, 3, 4)[4 * i + m]][:, :], 2),
                                         ACT.Copy, scale=sml[:, 128 + i:129 + i]).then_inc(S("turn_out"), 1)

            def attention(a, oT, gate=None):
                for n in range(10):
                    if n < 8:
                        h = 8 * a + n
                        act.wait_ge(S("max_done"), h + 1)
                        for b, (x, y) in enumerate(((0, P), (P, DIAG))):
                            at = 136 + 2 * (n % 2) + b
                            nc.scalar.activation(p_sb[n % 2][:, x:y], sc_sb[n % 2][:, x:y], ACT.Exp,
                                                 scale=-1.0, bias=sml[:, at:at + 1],
                                                 accum_out=sml[:, at + 4:at + 5])\
                                .then_inc(S("exp_done"), 1)
                    if gate is not None:
                        gate(n)
                    if 1 <= n < 9:
                        h = 8 * a + n - 1
                        act.wait_ge(S("p_turned"), h + 1)
                        nc.scalar.activation(pt_sb[(n - 1) % 2], pb[2 + (n - 1) % 2][:, 0:DIAG], ACT.Copy)\
                            .then_inc(S("pt_out"), 1)
                    if n >= 2:
                        h = 8 * a + n - 2
                        act.wait_ge(S("o_done"), h + 1)
                        nc.scalar.activation(oT[:, n - 2, :], pb[4 + n % 2][:, 0:T], ACT.Copy)\
                            .then_inc(S("o_out"), 1)

            def values_out(n):
                if n in (4, 8):
                    rows_out(9 + n // 4)

            attention(0, a_oT, values_out)
            squares(3)
            root(6, 3, pb[0][:, 0:T], D)
            tables(SILU)
            ffn(1)

            def bias_copies():
                for m in range(2):
                    act.wait_ge(S("bias_turned"), m + 1)
                    for half in range(2):
                        src = three(pb[2 * m + half][:, :], 2)
                        dst = biasT[:, 4 * m + 2 * half:4 * m + 2 * half + 2, :]
                        nc.scalar.activation(dst[:, :, 0:P], src[:, :, P:T], ACT.Copy, scale=KV_LORA ** 0.5)\
                            .then_inc(S("bias_cp"), 1)
                        nc.scalar.activation(dst[:, :, P:DIAG], src, ACT.Copy, scale=KV_LORA ** 0.5)\
                            .then_inc(S("bias_cp"), 1)

            def layer(l):
                nn, ns = 7 + 4 * l, 4 + 4 * l
                squares(4 + l)
                root(nn, ns, pb[7][:, 0:T], D)
                if l == 0:
                    bias_copies()
                for k in range(DC):
                    act.wait_ge(S("xn_done"), 8 * l + k + 1)
                    nc.scalar.activation(xg[:, k, :], xg[:, k, :], ACT.Identity, bias=mod[:, l, k:k + 1])\
                        .then_inc(S("xs_done"), 1)
                product(act, 32 + 16 * l)
                bank = three(pb[0][:, :], 2)
                nc.scalar.activation(b_cq, bank, ACT.Copy).then_inc(S("cq_out"), 1)
                nc.scalar.activation(sq[:, 0:2, :], bank, ACT.Square).then_inc(S("cq_out"), 1)
                product(act, 33 + 16 * l)
                nc.scalar.activation(b_kv, pb[1][:, 0:T], ACT.Copy).then_inc(S("cq_out"), 1)
                nc.scalar.activation(sq[:, 2, :], pb[1][:, 0:T], ACT.Square).then_inc(S("cq_out"), 1)
                nc.scalar.activation(b_kidx[0:64, :], pb[1][0:64, T:2 * T], ACT.Copy).then_inc(S("cq_out"), 1)
                nc.scalar.activation(widx_row[64:72, :], pb[1][64:72, T:2 * T], ACT.Copy)\
                    .then_inc(S("cq_out"), 1)
                act.wait_ge(S("cq_out"), 6 * l + 5)
                act.dma_start(b_kidx[64:P, :], b_kidx[0:64, :]).then_inc(S("kidx_in"), 16)
                act.wait_ge(S("ss_done"), ns + 2)
                after(link(nc.scalar.activation(lny[:, 0:T], pb[3][:, 0:T], ACT.Ln, scale=1.0 / 256,
                                                bias=sml[:, 180:181])))
                nc.scalar.activation(lny[:, T:2 * T], pb[3][:, T:2 * T], ACT.Ln, scale=1.0 / 128,
                                     bias=sml[:, 180:181]).then_inc(S("ln_done"), 1)
                act.wait_ge(S("ln_done"), lns(ns + 1))
                guess(nn + 1, lny[:, :], rstd[:, :])
                tables(SIGMOID)
                product(act, 35 + 16 * l)
                if l > 0:
                    act.wait_ge(S("glu_done"), 2 * l)
                nc.scalar.activation(b_sg, three(pb[1][:, :], 2), ACT.Sigmoid).then_inc(S("glu_gate"), 1)
                act.wait_ge(S("kv_turned"), l + 1)
                nc.scalar.activation(b_kvt, three(pb[3][:, 0:T], 2), ACT.Copy).then_inc(S("kvt_out"), 1)

                def tap0(i):
                    act.wait_ge(S("glu_done"), 2 * l + i + 1)
                    if l > 0:
                        act.wait_ge(S("yn_done"), l)
                    for c in (2 * i, 2 * i + 1):
                        nc.scalar.activation(b_y[:, c, :], b_a[:, c, 0:T], ACT.Identity,
                                             bias=col("conv_b_2", 4 * l + c),
                                             scale=col("conv_w_2", 124 * l + c)).then_inc(S("conv0_done"), 1)

                tap0(0)
                product(act, 36 + 16 * l)
                for m in range(4):
                    nc.scalar.activation(b_qT[:, 2 * m:2 * m + 2, :], three(pb[4 + m][:, :], 2), ACT.Copy)\
                        .then_inc(S("uq_out"), 1)
                for m in range(2):
                    act.wait_ge(S("qi_proj"), 2 * l + m + 1)
                    nc.scalar.activation(b_qi[:, 2 * m:2 * m + 2, :], three(pb[2 + m][:, :], 2), ACT.Copy)\
                        .then_inc(S("qi_out"), 1)
                for r in range(6):
                    act.wait_ge(S("idx_done"), 6 * l + r + 1)
                    if r >= 2 or l > 0:
                        act.wait_ge(S("relu_read"), 6 * l + r - 1)
                    nc.scalar.activation(relu[r % 2], pb[(4, 5, 6, 7, 2, 3)[r]][:, :], ACT.Relu)\
                        .then_inc(S("relu_done"), 1)
                product(act, 38 + 16 * l)
                act.wait_ge(S("glu_done"), 2 * l + 1)
                nc.scalar.activation(b_sg, three(pb[1][:, :], 2), ACT.Sigmoid).then_inc(S("glu_gate"), 1)
                tap0(1)
                tables(LN_EXP)

                def gate(n_head):
                    if n_head % 2 == 0 and n_head >= 2:
                        m = n_head // 2 - 1
                        product(act, 39 + 16 * l + m)
                        nc.scalar.activation(y2[:, 2 * m:2 * m + 2, :], three(pb[6 + m % 2][:, :], 2), ACT.Copy)\
                            .then_inc(S("gates_cp"), 1)
                    if n_head == 8:
                        tables(SILU)

                attention(1 + l, b_oT, gate)
                act.wait_ge(S("gates_cp"), 4 * l + 4)
                for half in (1, 0):
                    x = y2[:, 4 * half:4 * half + 4, :]
                    nc.scalar.activation(x, x, ACT.Silu).then_inc(S("gates_out"), 1)
                tables(LN_EXP)
                act.wait_ge(S("yn_done"), l + 1)
                nc.scalar.activation(sq[:, 0:4, :], b_yn, ACT.Square).then_inc(S("ynsq_done"), 1)
                root(nn + 2, ns + 3, pb[3][:, 0:T], D_CONV)
                tables(SILU)
                for c in range(CC):
                    act.wait_ge(S("z_done"), CC * l + c + 1)
                    nc.scalar.activation(b_z[:, c, :], b_z[:, c, :], ACT.Silu,
                                         bias=col("conv_ln_b_2", 4 * l + c)).then_inc(S("zs_done"), 1)
                tables(LN_EXP)
                for j in range(2):
                    for b in range(TB):
                        if b == 0:
                            act.wait_ge(S("mix_done"), 2 * l + j + 1)
                        else:
                            product(act, 45 + 16 * l + 2 * j)
                        bank = pb[4 + 2 * j + b][:, :]
                        nc.scalar.activation(sq[:, 4 * j + 2 * b:4 * j + 2 * b + 2, :].rearrange("p a b -> p (a b)"), bank,
                                             ACT.Square, accum_out=sml[:, 2 * j + b:2 * j + b + 1])\
                            .then_inc(S("out_sq"), 1)
                        nc.scalar.activation(b_ytok[:, b, 512 * j:512 * j + 512], bank, ACT.Copy)\
                            .then_inc(S("out_cp"), 1)
                root_of_ms(nn + 3, sml[:, 4:6], sml[:, 6:8], sml[:, 8:10])

            for l in range(DEPTH):
                layer(l)
            for half in range(2):
                for b in range(TB):
                    act.wait_ge(S("h_turned"), 2 * half + b + 1)
                    nc.scalar.activation(y_rows[:, b, 512 * half:512 * half + 512], pb[4 + 2 * b + half][:, :],
                                         ACT.Copy).then_inc(S("y_cp"), 1)

        @block.tensor
        def _(pe):
            mm = nc.tensor.matmul

            def feat(n, bank, x, w=None, nk=DC, chunks=2, at=0, x_ready=None, last_of_slot=True):
                w = slot8(n) if w is None else w
                arrived(pe, n)
                for c in range(chunks):
                    for k in range(nk):
                        if c == 0 and x_ready is not None:
                            x_ready(k)
                        last = mm(bank[:, T * c:T * (c + 1)], w[:, k, at + P * c:at + P * (c + 1)], x[:, k, :],
                                  start=(k == 0), stop=(k == nk - 1))
                return last.then_inc(S("product"), 1) if last_of_slot else last

            def token(n, bank, x, x_ready=None):
                arrived(pe, n)
                for b in range(TB):
                    for k in range(DC):
                        if b == 0 and x_ready is not None:
                            x_ready(k)
                        last = mm(bank[:, T * b:T * (b + 1)], x[:, k, P * b:P * (b + 1)], slot8(n)[:, k, :],
                                  start=(k == 0), stop=(k == DC - 1))
                last.then_inc(S("product"), 1)

            def ss(n, bank, src=None):
                pe.wait_ge(S("sum_done"), n + 1)
                mm(bank, ones[:, 0:P], sq[:, 0, :] if src is None else src, start=True, stop=True)\
                    .then_inc(S("ss_done"), 1)

            def token_rstd(bank):
                for b in range(TB):
                    last = nc.tensor.transpose(bank[:, P * b:P * (b + 1)], rstd[:, P * b:P * (b + 1)], ident)
                last.then_inc(S("rcol_turned"), 1)

            def xg_ready(base):
                return lambda k: pe.wait_ge(S("xg_ready"), base + k + 1)

            pe.wait_ge(S("ident_in"), 16)
            pe.wait_ge(S("x_in"), 32)
            for m in range(4):
                for c in range(2):
                    for b in range(TB):
                        last = nc.tensor.transpose(pb[m][:, T * c + P * b:T * c + P * b + P],
                                                   x_rows[:, b, P * (2 * m + c):P * (2 * m + c + 1)], ident)
                last.then_inc(S("x_turned"), 1)
            pe.wait_ge(S("a_in"), 16)
            nc.tensor.transpose(pb[7][:, 0:8], a_norm_rows, ident[0:8, 0:8]).then_inc(S("a_norm_turned"), 1)

            pe.wait_ge(S("ones_set"), 2)
            feat(0, pb[0], xg, x_ready=xg_ready(0))
            feat(1, pb[1], xg)
            pe.wait_ge(S("param_in"), 16 * len(PIECES))
            for bank, r0, r1 in ((pb[4], 0, 4), (pb[5], 4, NTURN)):
                for r in range(r0, r1):
                    last = nc.tensor.transpose(bank[:, P * (r - r0):P * (r - r0 + 1)], pstage[:, r, :], ident)
                last.then_inc(S("params_turned"), 1)
            pe.wait_ge(S("cols_done"), 2)
            ss(0, pb[5][:, 0:T])
            pe.wait_ge(S("rb_in"), 16)
            pe.wait_ge(S("const_in"), 16)
            mm(pb[6][0:8, 0:3 * P], sml[0:BUCKETS, 161:169], pc("bucket", 3 * P)[0:BUCKETS, :],
               start=True, stop=True).then_inc(S("rowsT_done"), 1)
            feat(2, pb[2], xg)
            feat(3, pb[3], xg)
            pe.wait_ge(S("gw_in"), 32)
            for k in range(DC):
                last = mm(pb[4][0:64, 0:T], m_gw[:, k, :], xg[:, k, :], start=(k == 0), stop=(k == DC - 1))
            last.then_inc(S("m_gate_proj"), 1)
            pe.wait_ge(S("rstd_done"), 1)
            token_rstd(pb[5])
            pe.wait_ge(S("rows_done"), 1)
            token(4, pb[6], xg)
            token(5, pb[7], xg)
            pe.wait_ge(S("m_q_out"), 2)
            token(6, pb[0], xg)
            token(7, pb[1], xg)
            pe.wait_ge(S("m_rows_done"), 1)
            pe.wait_ge(S("rcol_done"), 1)
            for b in range(TB):
                last = nc.tensor.transpose(pb[5][:, 4 * b:4 * b + 4], rows[0:4, 5, P * b:P * (b + 1)],
                                           pc("ident", 4)[0:4, :])
            last.then_inc(S("ccol_turned"), 1)
            head_row = pc("head_row", 4 * P)[0:4, :]

            def spread(h, row, sem):
                last = mm(pb[4 + h // 2][:, T * (h % 2):T * (h % 2 + 1)], head_row[:, P * h:P * (h + 1)], row,
                          start=True, stop=True)
                if h % 2:
                    last.then_inc(S(sem), 1)

            spread(0, rows[0:4, 6, :], "m_spread")
            spread(1, rows[0:4, 6, :], "m_spread")
            pe.wait_ge(S("ccol_done"), 1)
            spread(2, rows[0:4, 6, :], "m_spread")
            spread(3, rows[0:4, 6, :], "m_spread")

            def m_scores(h):
                if h == 0:
                    pe.wait_ge(S("m_k_out"), 2)
                if h >= 2:
                    pe.wait_ge(S("m_p"), h - 1)
                bank = pb[2 + h % 2]
                mm(bank[:, 0:T], m_k[:, h, 0:P], m_q[:, h, :], start=True, stop=True)
                mm(bank[:, T:DIAG], m_k[:, h, P:T], m_q[:, h, P:T], start=True, stop=True)\
                    .then_inc(S("m_scores"), 1)

            def m_square_sum(h):
                pe.wait_ge(S("m_sqs"), h + 1)
                mm(pb[6][0:4, T:2 * T], pc("head_col", 16)[:, 4 * h:4 * h + 4], m_sqn[:, 2 * (h % 2), :],
                   start=False, stop=(h == 3), skip_group_check=True).then_inc(S("m_sums"), 1)

            m_scores(0)
            m_scores(1)
            for h in range(M_HEADS):
                if h == 0:
                    pe.wait_ge(S("m_v_out"), 8)
                if h < 3:
                    if h > 0:
                        pe.wait_ge(S("m_o_scaled"), h)
                    feat(8 + h, pb[7], xg)
                pe.wait_ge(S("m_p"), h + 1)
                pt = m_pt[h % 2]
                sel = pc("head_col", 16)[:, 4 * h:4 * h + 4]
                mm(pb[6][0:4, 0:T], sel, pt[:, 0:T], start=(h == 0), stop=False, skip_group_check=True)
                mm(pb[6][0:4, P:T], sel, pt[:, T:DIAG], start=False, stop=(h == 3), skip_group_check=True)
                if h >= 2:
                    pe.wait_ge(S("m_num_out"), 2 * (h - 1))
                for c in range(2):
                    o = T * c
                    at = M_DV * h + P * c
                    mm(pb[h % 2][:, o:o + T], m_v[:, 0, at:at + P], pt[:, 0:T], start=True, stop=False)
                    last = mm(pb[h % 2][:, o + P:o + T], m_v[:, 1, at:at + P], pt[:, T:DIAG],
                              start=False, stop=True)
                last.then_inc(S("m_num_done"), 1)
                if h < 2:
                    m_scores(h + 2)
                if h >= 1:
                    m_square_sum(h - 1)
            m_square_sum(3)
            pe.wait_ge(S("m_o_scaled"), 3)
            feat(11, pb[7], xg)
            pe.wait_ge(S("rstd_done"), 2)
            for h in range(4):
                spread(h, rows[0:4, 7, :], "f_spread")
            pe.wait_ge(S("m_num_out"), 8)
            for m in range(4):
                feat(12 + m, pb[m], m_y,
                     x_ready=(lambda k: pe.wait_ge(S("m_y_done"), k // 2 + 1)) if m == 0 else None)

            def turn_ada(f, m):
                if m >= 4:
                    pe.wait_ge(S("mod_red"), 6 * f + m - 3)
                for c in range(4):
                    last = nc.tensor.transpose(pb[4 + m % 4][:, P * c:P * (c + 1)],
                                               f_acc[:, P * (4 * m + c):P * (4 * m + c + 1)], ident)
                last.then_inc(S("ada_turned"), 1)

            def ffn(f, nth):
                g0 = FF_STEPS * f

                def up(g, par, turn, x_ready=None):
                    if x_ready is None:
                        pe.wait_ge(S("u_ready"), g - 1)
                    pe.wait_ge(S(f"f_up{par}"), 32 * turn)
                    for j in range(2):
                        w = fring[:, par, j, :].rearrange("p (k n) -> p k n", k=8)
                        for c in range(2):
                            for k in range(DC):
                                if x_ready is not None and j == 0 and c == 0:
                                    x_ready(k)
                                last = mm(pb[4 + 2 * par + j][:, T * c:T * (c + 1)], w[:, k, P * c:P * (c + 1)],
                                          xg[:, k, :], start=(k == 0), stop=(k == DC - 1))
                    last.then_inc(S("up_done"), 1)

                def down(g, par, turn, first=False, end=False):
                    pe.wait_ge(S(f"f_down{par}"), 16 * turn)
                    pe.wait_ge(S("act_ready"), g + 1)
                    w = fring[:, par, 2, :].rearrange("p (k n) -> p k n", k=2)
                    for k in range(2):
                        for m in range(DC):
                            last = mm(pb[m // 2][:, T * (m % 2):T * (m % 2 + 1)], w[:, k, P * m:P * (m + 1)],
                                      f_act[:, par, T * k:T * (k + 1)],
                                      start=(first and k == 0 and m % 2 == 0), stop=(end and k == 1),
                                      skip_group_check=True)
                            if end and k == 1 and m in (1, 3, 5):
                                last.then_inc(S("out_bank"), 1)
                    last.then_inc(S("down_done"), 1)

                p = g0 % 2
                up(g0, p, g0 // 2 + 1, x_ready=xg_ready(8 + 16 * f))
                ss(nth, pb[0][:, 0:T])
                up(g0 + 1, 1 - p, (g0 + 1) // 2 + 1, x_ready=lambda k: None)
                down(g0, p, g0 // 2 + 1, first=True)
                with pe.Fori(0, 4) as j:
                    for s in range(2):
                        g = 2 * j + (g0 + s + 2)
                        up(g, (g0 + s) % 2, j + ((g0 + s) // 2 + 2))
                        down(g - 1, (g0 + s + 1) % 2, j + ((g0 + s - 1) // 2 + 2))
                g = g0 + FF_STEPS - 1
                up(g, g % 2, g // 2 + 1)
                down(g - 1, (g - 1) % 2, (g - 1) // 2 + 1)
                pe.wait_ge(S("u_ready"), g + 1)
                pe.wait_ge(S("ada_free"), 2 + 16 * (f + 1))
                for m in range(4):
                    turn_ada(f, m)
                down(g, g % 2, g // 2 + 1, end=True)
                for m in (4, 5):
                    turn_ada(f, m)

            ffn(0, 1)

            def attention(a, q, k, v, between=None):
                for n in range(10):
                    if between is not None and n == 0:
                        between(n)
                    if n < 8:
                        h = 8 * a + n
                        if n >= 2:
                            pe.wait_ge(S("max_done"), h - 1)
                        bank = pb[n % 2]
                        mm(bank[:, 0:P], q[:, n, 0:P], k(n)[:, 0:P], start=True, stop=True)
                        mm(bank[:, P:DIAG], q[:, n, P:T], k(n)[:, 0:T], start=True, stop=True)\
                            .then_inc(S("scores_done"), 1)
                    if between is not None and n > 0:
                        between(n)
                    if 1 <= n < 9:
                        h = 8 * a + n - 1
                        pe.wait_ge(S("p_ready"), h + 1)
                        if n >= 3:
                            pe.wait_ge(S("pt_out"), h - 1)
                        bank = pb[2 + (n - 1) % 2]
                        for x in (0, P, 2 * P):
                            last = nc.tensor.transpose(bank[:, x:x + P], p_sb[(n - 1) % 2][:, x:x + P], ident)
                        last.then_inc(S("p_turned"), 1)
                    if n >= 2:
                        h = 8 * a + n - 2
                        pe.wait_ge(S("pt_out"), h + 1)
                        if n >= 4:
                            pe.wait_ge(S("o_out"), h - 1)
                        pt = pt_sb[n % 2]
                        bank = pb[4 + n % 2]
                        mm(bank[:, 0:T], v(0, n - 2), pt[:, 0:T], start=True, stop=False)
                        mm(bank[:, P:T], v(1, n - 2), pt[:, T:DIAG], start=False, stop=True)\
                            .then_inc(S("o_done"), 1)

            token(16, pb[0], xg, x_ready=xg_ready(16))
            pe.wait_ge(S("mod_red"), 4)
            ss(2, pb[7][:, 0:T])
            token(17, pb[1], xg)
            pe.wait_ge(S("mod_red"), 6)
            pe.wait_ge(S("rstd_done"), 4)
            token_rstd(pb[7])
            token(18, pb[2], xg)
            token(19, pb[3], xg)
            token(20, pb[4], a_xq, x_ready=lambda k: pe.wait_ge(S("xq_ready"), k + 1))
            token(21, pb[5], a_xq)
            token(22, pb[6], a_xq)
            for s, bank in ((7, 0), (8, 1), (9, 2)):
                pe.wait_ge(S("tok_out"), 2 * (s - 7) + 2)
                token(16 + s, pb[bank], a_xq if s == 7 else xg)
            for i, src in ((0, a_kt), (1, a_qt)):
                pe.wait_ge(S("rot_done"), i + 1)
                for m in range(4):
                    if i == 0 and m == 0:
                        pe.wait_ge(S("tok_out"), 16)
                        pe.wait_ge(S("rcol_done"), 2)
                    if i == 1 and m == 0:
                        pe.wait_ge(S("tok_out"), 20)
                    bank = pb[(5, 6, 7, 0, 1, 2, 3, 4)[4 * i + m]]
                    for c in range(2):
                        for b in range(TB):
                            h = 2 * m + c
                            last = nc.tensor.transpose(bank[:, T * c + P * b:T * c + P * (b + 1)],
                                                       src[:, b, P * h:P * (h + 1)], ident)
                    last.then_inc(S("a_turned"), 1)

            def values(n):
                if n < 8:
                    i, b, half = n // 4, n // 2 % 2, n % 2
                    if n == 0:
                        arrived(pe, 26)
                        pe.wait_ge(S("turn_out"), 3)
                    if n == 4:
                        arrived(pe, 27)
                    for k in range(4 * half, 4 * half + 4):
                        last = mm(pb[6 + i][:, T * b:T * (b + 1)], xg[:, k, P * b:P * (b + 1)],
                                  slot8(26 + i)[:, k, :], start=(k == 0), stop=(k == DC - 1),
                                  skip_group_check=True)
                    if n % 4 == 3:
                        last.then_inc(S("product"), 1)
                if n == 0:
                    pe.wait_ge(S("turn_out"), 8)
                if n >= 2:
                    pe.wait_ge(S("tok_out"), 2 * (9 + (n - 2) // 2))

            attention(0, a_qT, lambda h: a_kT[:, h, :], lambda b, h: a_v[:, b, A_DH * h:A_DH * (h + 1)], values)
            for m in range(4):
                if m == 0:
                    pe.wait_ge(S("o_out"), 8)
                feat(28 + m, pb[m], a_oT)

            ffn(1, 3)

            pe.wait_ge(S("skew_in"), 16)
            pe.wait_ge(S("h_ready"), 20)
            skew_f = skew.rearrange("p h t -> p (h t)")
            for m in range(4):
                last = mm(pb[m][:, :], pc("flip", P), skew_f[:, 512 * m:512 * m + 512], start=True, stop=True)
                if m % 2:
                    last.then_inc(S("bias_turned"), 1)
            pe.wait_ge(S("mod_red"), 12)

            def layer(l):
                n = 32 + 16 * l
                nn = 7 + 4 * l
                ns = 4 + 4 * l
                ss(ns, pb[7][:, 0:T])
                pe.wait_ge(S("bias_cp"), 8)
                feat(n, pb[0], xg, x_ready=lambda k: pe.wait_ge(S("xs_done"), 8 * l + k + 1))
                arrived(pe, n + 1)
                for at, wide in ((0, P), (P, 72)):
                    for k in range(DC):
                        last = mm(pb[1][0:wide, 2 * at:2 * at + T], slot8(n + 1)[:, k, at:at + wide], xg[:, k, :],
                                  start=(k == 0), stop=(k == DC - 1))
                last.then_inc(S("product"), 1)
                pe.wait_ge(S("cq_out"), 6 * l + 2)
                feat(n + 2, pb[0], xg)
                ss(ns + 1, pb[3][:, :], src=sq[:, 1:3, :].rearrange("p a b -> p (a b)"))
                pe.wait_ge(S("cq_out"), 6 * l + 6)
                feat(n + 3, pb[1], xg)
                for b in range(TB):
                    last = nc.tensor.transpose(pb[2][:, 8 * b:8 * b + 8], widx_row[64:72, P * b:P * (b + 1)],
                                               ident[64:72, 64:72])
                last.then_inc(S("wcol_turned"), 1)
                pe.wait_ge(S("cqn_done"), l + 1)
                for b in range(TB):
                    last = nc.tensor.transpose(pb[3][:, P * b:P * (b + 1)], b_kvn[:, P * b:P * (b + 1)], ident)
                last.then_inc(S("kv_turned"), 1)
                arrived(pe, n + 4)
                pe.wait_ge(S("small_in"), 32 * (l + 1))
                w_uq = slot(n + 4).rearrange("p (k n) -> p k n", k=2)
                for m in range(4):
                    feat(n + 4, pb[4 + m], b_cqn, w=w_uq, nk=2, at=256 * m, last_of_slot=(m == 3))
                pe.wait_ge(S("wcol_done"), l + 1)
                feat(n + 4, pb[2], b_cqn, w=w_qidx, nk=2, at=0, last_of_slot=False).then_inc(S("qi_proj"), 1)
                pe.wait_ge(S("kvt_out"), l + 1)
                feat(n + 4, pb[3], b_cqn, w=w_qidx, nk=2, at=256, last_of_slot=False)\
                    .then_inc(S("qi_proj"), 1)
                pe.wait_ge(S("uq_out"), 4 * l + 4)
                pe.wait_ge(S("qi_out"), 2 * l + 2)
                pe.wait_ge(S("kidx_in"), 16 * (l + 1))
                for r, heads in enumerate(IDX_ORDER):
                    b = 1 if r < 4 else 0
                    wide = P * (b + 1)
                    for i, h in enumerate(heads):
                        o = 64 * (h % 2)
                        last = mm(pb[(4, 5, 6, 7, 2, 3)[r]][:, wide * i:wide * (i + 1)],
                                  b_qi[o:o + 64, h // 2, P * b:P * (b + 1)], b_kidx[o:o + 64, 0:wide],
                                  start=True, stop=True)
                    last.then_inc(S("idx_done"), 1)
                pe.wait_ge(S("glu_done"), 2 * l + 1)
                feat(n + 5, pb[0], xg)
                feat(n + 6, pb[1], xg)
                pe.wait_ge(S("relu_done"), 6 * l + 6)

                def uv(m):
                    pe.wait_ge(S("o_out"), 8 * (1 + l) + 4 * m + 4)
                    pe.wait_ge(S("max_done"), 8 * (1 + l) + 7 + m)
                    for i in range(2):
                        for half in range(2):
                            h = 4 * m + 2 * i + half
                            last = mm(pb[m][64 * half:64 * half + 64, T * i:T * (i + 1)], w_uv[:, h, :],
                                      b_oT[:, h, :], start=True, stop=True)
                    last.then_inc(S("uv_done"), 1)

                def gates(n_head):
                    if n_head == 8:
                        uv(0)
                    if n_head >= 8:
                        return
                    m, c = n_head // 2, n_head % 2
                    if m >= 2 and c == 0:
                        pe.wait_ge(S("gates_cp"), 4 * l + m - 1)
                    last = feat(n + 7 + m, pb[6 + m % 2][:, T * c:T * (c + 1)], xg, chunks=1, at=P * c,
                                last_of_slot=(c == 1))
                    if n_head == 0:
                        pe.wait_ge(S("glu_done"), 2 * l + 2)

                attention(1 + l, b_qT, lambda h: b_kvn, lambda b, h: b_kvt[:, b, :], gates)
                uv(1)

                def mix(j, b, half):
                    bank = pb[4 + 2 * j + b]
                    for m in range(2):
                        load = n + 12 + 2 * j + m
                        if half == 1 and b == 0:
                            arrived(pe, load)
                        for k in range(4 * half, 4 * half + 4):
                            if j == 0 and b == 0 and m == 0 and k % 2 == 0:
                                if half == 1:
                                    pe.wait_ge(S("y2_attn"), 2 * l + k // 2 - 1)
                                else:
                                    pe.wait_ge(S("y2_conv"), 2 * l + k // 2 + 1)
                            last = mm(bank[:, T * m:T * (m + 1)], y2[:, k, P * b:P * (b + 1)],
                                      slot8(load)[:, k, :], start=(half == 1 and m == 0 and k == 4),
                                      stop=(half == 0 and k == 3), skip_group_check=True)
                        if half == 0 and b == 1:
                            last.then_inc(S("product"), 1)
                    if half == 0 and b == 0:
                        last.then_inc(S("mix_done"), 1)

                pe.wait_ge(S("o_out"), 8 * (2 + l))
                pe.wait_ge(S("gates_cp"), 4 * l + 4)
                mix(0, 0, 1)
                ss(ns + 2, pb[2][:, 0:T])
                mix(0, 1, 1)
                ss(ns + 3, pb[3][:, 0:T])
                mix(1, 0, 1)
                mix(1, 1, 1)
                w_pw2 = slot(n + 11).rearrange("p (k n) -> p k n", k=CC)
                feat(n + 11, pb[0], b_z, w=w_pw2, nk=CC, at=0, last_of_slot=False,
                     x_ready=lambda k: pe.wait_ge(S("zs_done"), CC * l + k + 1)).then_inc(S("pw2_first"), 1)
                feat(n + 11, pb[1], b_z, w=w_pw2, nk=CC, at=256)
                for j in range(2):
                    for b in range(TB):
                        mix(j, b, 0)
                for m in range(4):
                    for c in range(2):
                        for b in range(TB):
                            if m == 0 and c == 0:
                                pe.wait_ge(S("diag_done"), 2 * l + b + 1)
                            if m == 2 and c == 0 and b == 0:
                                pe.wait_ge(S("out_cp"), 4 * l + 4)
                            at = 256 * m + P * c
                            last = mm(pb[m][:, T * c + P * b:T * c + P * (b + 1)], b_ytok[:, b, at:at + P],
                                      diag[:, b, :], start=True, stop=True)
                    last.then_inc(S("y_turned"), 1)

            for l in range(DEPTH):
                layer(l)
            for half in range(2):
                for b in range(TB):
                    for c in range(4):
                        if b == 0 and c % 2 == 0:
                            pe.wait_ge(S("h_ready"), 24 + 2 * half + c // 2 + 1)
                        last = nc.tensor.transpose(pb[4 + 2 * b + half][:, P * c:P * (c + 1)],
                                                   hT[:, 4 * half + c, P * b:P * (b + 1)], ident)
                    last.then_inc(S("h_turned"), 1)

        @block.vector
        def _(dve):
            v = nc.vector
            done = [0, 0]

            def link(ins):
                ins.then_inc(S("dve_step"), 1)
                done[1] += 1
                return done[0] + done[1]

            def after(n):
                dve.wait_ge(S("dve_step"), n)

            def then(ins):
                after(link(ins))

            def mean_square(n, bank, dst, size):
                dve.wait_ge(S("ln_done"), lns(n))
                then(v.tensor_scalar(dst, bank, -0.5 / size, -0.5 * EPS, ALU.mult, ALU.add))

            def newton(nn, a, y, t, by=None):
                dve.wait_ge(S("guess_done"), nn + 1)
                then(v.tensor_tensor(t, y, a, ALU.mult))
                then(v.tensor_tensor(t, t, y, ALU.mult))
                if by is not None:
                    then(v.tensor_tensor(y, y, by, ALU.mult))
                v.scalar_tensor_tensor(y, t, 1.5, y, ALU.add, ALU.mult).then_inc(S("rstd_done"), 1)
                dve.wait_ge(S("rstd_done"), nn + 1)

            def fold(x, n, last):
                while n > 2:
                    n //= 2
                    then(v.tensor_tensor(x[:, 0:n, :], x[:, 0:n, :], x[:, n:2 * n, :], ALU.add))
                v.tensor_tensor(x[:, 0, :], x[:, 0, :], x[:, 1, :], ALU.add).then_inc(S(last), 1)

            def gained(k, dst, name, sem, at=0, pairs=range(4)):
                for c in range(2 * pairs[0], 2 * pairs[-1] + 2):
                    if c % 2 == 0:
                        dve.wait_ge(S("h_ready"), 4 * k + c // 2 + 1)
                    v.tensor_scalar(dst[:, c, :], hT[:, c, :], col(name, at + c), None, ALU.mult)\
                        .then_inc(S(sem), 1)

            def fold_pairs(sem, base):
                for m in range(1, 4):
                    dve.wait_ge(S(sem), base + m + 1)
                    then(v.tensor_tensor(sq[:, 0:2, :], sq[:, 0:2, :], sq[:, 2 * m:2 * m + 2, :], ALU.add))
                v.tensor_tensor(sq[:, 0, :], sq[:, 0, :], sq[:, 1, :], ALU.add).then_inc(S("sum_done"), 1)

            def residual_norm(k):
                fold_pairs("sq_done", 4 * k)

            def add_pair(m, bank):
                x = hT[:, 2 * m:2 * m + 2, :]
                v.tensor_tensor(x, x, three(bank[:, :], 2), ALU.add).then_inc(S("h_ready"), 1)

            for m in range(4):
                dve.wait_ge(S("x_turned"), m + 1)
                v.tensor_copy(hT[:, 2 * m:2 * m + 2, :], three(pb[m][:, :], 2)).then_inc(S("h_ready"), 1)
            dve.wait_ge(S("a_norm_turned"), 1)
            then(v.tensor_copy(a_norm_cols, pb[7][:, 0:8]))
            for c in range(DC):
                v.tensor_scalar(xg[:, c, :], hT[:, c, :], a_norm_cols[:, c:c + 1], None, ALU.mult)\
                    .then_inc(S("xg_ready"), 1)
            residual_norm(0)
            dve.wait_ge(S("cols_done"), 2)
            then(v.tensor_copy(sml[:, 128:129], cols[:, COLS["k_norm"][0]:COLS["k_norm"][0] + 1]))
            then(v.tensor_copy(sml[:, 129:130], cols[:, COLS["b_q_norm"][0]:COLS["b_q_norm"][0] + 1]))
            v.memset(sml[0:ROT, 128:130], 1.0).then_inc(S("ada_free"), 2)

            mean_square(0, pb[5][:, 0:T], ms[:, 0:T], D)
            newton(0, ms[:, 0:T], rbc, nwt[:, 0:T])
            for m in range(4):
                product(dve, m)
                dst = (m_q, m_k)[m // 2][:, 2 * (m % 2):2 * (m % 2) + 2, :]
                v.scalar_tensor_tensor(dst, three(pb[m][:, :], 2), M_DQK ** -0.5 if m < 2 else 1.0, rbc2,
                                       ALU.mult, ALU.mult).then_inc(S("m_q_out" if m < 2 else "m_k_out"), 1)
            dve.wait_ge(S("m_gate_proj"), 1)
            dve.wait_ge(S("gb_in"), 32)
            for a in (0, 32):
                r = rows[a:a + 4, 0, :]
                then(v.tensor_tensor(r, pb[4][a:a + 4, 0:T], rstd[a:a + 4, 0:T], ALU.mult))
                then(v.tensor_scalar(r, r, sml[a:a + 4, 160:161], None, ALU.add))
            f = rows[32:36, 0, :]
            v.scalar_tensor_tensor(rows[32:36, 1, :], f, -1.0, f, ALU.mult, ALU.max).then_inc(S("fabs_done"), 1)
            dve.wait_ge(S("rcol_turned"), 1)
            v.tensor_copy(rcol[:, 0:1], pb[5][:, 0:1])
            v.tensor_copy(rcol[:, 1:2], pb[5][:, P:P + 1]).then_inc(S("rcol_done"), 1)
            dve.wait_ge(S("fln_done"), 1)
            lf, B, c, M = rows[0:4, 1, :], rows[0:4, 4, :], rows[0:4, 5, :], rows[0:4, 6, :]
            then(v.scalar_tensor_tensor(lf, f, 0.0, rows[32:36, 3, :], ALU.min, ALU.subtract))
            then(v.tensor_tensor_scan(B, ones[0:4, :], lf, 0.0, ALU.mult, ALU.add))
            then(v.tensor_tensor(c, rows[0:4, 0, :], B, ALU.subtract))
            then(v.tensor_tensor_scan(M, c, c, 0.0, ALU.max, ALU.max))
            then(v.tensor_tensor(rows[0:4, 2, :], B, M, ALU.add))
            v.tensor_scalar(M, M, -1.0, None, ALU.mult).then_inc(S("m_rows_done"), 1)
            dve.wait_ge(S("ccol_turned"), 1)
            v.tensor_copy(sml[:, 0:8], pb[5][:, 0:8]).then_inc(S("ccol_done"), 1)

            def m_decay(h):
                dve.wait_ge(S("m_spread"), h // 2 + 1)
                if h >= 2:
                    dve.wait_ge(S("m_p"), h - 1)
                src = pb[4 + h // 2][:, T * (h % 2):T * (h % 2 + 1)]
                e = m_e[h % 2]
                v.tensor_tensor(e[:, 0:T], src, pc("mask_st", T), ALU.add)
                v.tensor_tensor(e[:, T:DIAG], src[:, P:T], pc("mask_st", P), ALU.add).then_inc(S("m_tmp"), 1)

            def m_output_gate(h):
                product(dve, 8 + h)
                v.tensor_tensor(m_o[:, 2 * h:2 * h + 2, :], three(pb[7][:, :], 2), rbc2, ALU.mult)\
                    .then_inc(S("m_o_scaled"), 1)

            m_decay(0)
            m_decay(1)
            for h in range(M_HEADS):
                dve.wait_ge(S("m_exp"), 2 * h + 2)
                dve.wait_ge(S("m_scores"), h + 1)
                if h >= 2:
                    dve.wait_ge(S("m_num_done"), h - 1)
                v.tensor_tensor(m_pt[h % 2], pb[2 + h % 2][:, 0:DIAG], m_e[h % 2], ALU.mult)\
                    .then_inc(S("m_p"), 1)
                if h < 2:
                    m_decay(h + 2)
                if h < 3:
                    m_output_gate(h)
                dve.wait_ge(S("m_num_out"), 2 * h + 2)
                x = m_sqn[:, 2 * (h % 2):2 * (h % 2) + 2, :]
                v.tensor_tensor(x[:, 0, :], x[:, 0, :], x[:, 1, :], ALU.add).then_inc(S("m_sqs"), 1)
            dve.wait_ge(S("m_sums"), 4)
            dve.wait_ge(S("floor_done"), 1)
            r0, r1 = rows[0:4, 0, :], rows[0:4, 1, :]
            then(v.tensor_copy(r0, pb[6][0:4, 0:T]))
            then(v.scalar_tensor_tensor(r0, r0, -1.0, r0, ALU.mult, ALU.max))
            then(v.tensor_tensor(r0, r0, rows[0:4, 3, :], ALU.max))
            then(v.reciprocal(r1, r0))
            then(v.tensor_tensor(r0, r1, r1, ALU.mult))
            then(v.tensor_tensor(r0, r0, pb[6][0:4, T:2 * T], ALU.mult))
            v.tensor_scalar(rows[0:4, 5, :], r0, 1.0 / M_DV, EPS, ALU.mult, ALU.add).then_inc(S("ms_done"), 1)
            a, y, t = rows[0:4, 5, :], rows[0:4, 7, :], rows[0:4, 2, :]
            dve.wait_ge(S("ms_done"), 1)
            dve.wait_ge(S("guess_done"), 2)
            then(v.tensor_scalar(a, a, -0.5, None, ALU.mult))
            newton(1, a, y, t, by=r1)
            m_output_gate(3)
            for h in range(M_HEADS):
                dve.wait_ge(S("f_spread"), h // 2 + 1)
                dve.wait_ge(S("m_num_out"), 8)
                x = m_num[:, 2 * h:2 * h + 2, :]
                src = pb[4 + h // 2][:, T * (h % 2):T * (h % 2 + 1)].unsqueeze(1).broadcast_to([P, 2, T])
                then(v.tensor_tensor(x, x, src, ALU.mult))
                dve.wait_ge(S("m_o_gate"), h + 1)
                product(dve, 11)
                for i in range(2):
                    c = 2 * h + i
                    ins = v.scalar_tensor_tensor(m_y[:, c, :], m_num[:, c, :], col("a_h_norm", c), m_o[:, c, :],
                                                 ALU.mult, ALU.mult)
                ins.then_inc(S("m_y_done"), 1)
            for m in range(4):
                product(dve, 12 + m)
                add_pair(m, pb[m])
            gained(1, xg, "f_norm", "xg_ready")

            def modulation(l, m0, m1):
                for m in range(m0, m1):
                    dve.wait_ge(S("ada_turned"), 6 * l + m + 1)
                    v.tensor_reduce(mod[:, l, 4 * m:4 * m + 4],
                                    pb[4 + m % 4][:, :].rearrange("p (c k) -> p c k", c=4), AX.X, ALU.add)\
                        .then_inc(S("mod_red"), 1)
                if m1 < 6:
                    return
                dve.wait_ge(S("mod_red"), 6 * l + 6)
                a = COLS["b_ada_2"][0] + 24 * l
                then(v.tensor_tensor(mod[:, l, :], mod[:, l, :], cols[:, a:a + 24], ALU.add))

            def ffn(f, nth, nn):
                residual_norm(nth)
                g0 = FF_STEPS * f
                mean_square(nth, pb[0][:, 0:T], ms[:, 0:T], D)
                newton(nn, ms[:, 0:T], rbc, nwt[:, 0:T])

                def step(g, i, par, ada=None):
                    dve.wait_ge(S("up_done"), g + 1)
                    for q in range(2):
                        ins = v.tensor_tensor(f_u[:, q, :, 2:2 + T], three(pb[4 + 2 * par + q][:, :], 2), rbc2,
                                              ALU.mult)
                    ins.then_inc(S("u_ready"), 1)
                    dve.wait_ge(S("u_ready"), g + 1)
                    for tap in (1, 2):
                        marks = [] if tap == 1 else marks
                        new = []
                        for q in (1, 0):
                            for c in range(2):
                                n = 22 * q + 2 * i + c
                                if tap == 1 and c == 0:
                                    dve.wait_ge(S("tap0_done"), 4 * g + 2 * q + 2)
                                if tap == 2:
                                    after(marks[len(new)])
                                ins = v.scalar_tensor_tensor(f_t[q][:, c, :], f_u[:, q, c, tap:tap + T],
                                                             col(f"f_conv_w{f}", 44 * tap + n), f_t[q][:, c, :],
                                                             ALU.mult, ALU.add)
                                if tap == 2 and q == 1 and c == 1:
                                    ins.then_inc(S("gate_conv"), 1)
                                    new.append(None)
                                else:
                                    new.append(link(ins))
                        marks = new
                    if ada is not None:
                        for half in range(2):
                            dve.wait_ge(S(f"ada{half}"), ada + 16 * 8 * f)
                            acc = f_acc[:, 1536 * half:1536 * half + 1536]
                            k = cact[:, bass.ds(i - 2, 1)]
                            ins = v.scalar_tensor_tensor(acc, f_ada[:, half, :], k, acc, ALU.mult, ALU.add)
                            ins.then_inc(S("ada_free"), 1)
                            dve.wait_ge(S("ada_free"), ada_turn(g, half))
                    dve.wait_ge(S("silu_done"), g + 1)
                    after(marks[3])
                    if not isinstance(g, int) or g >= 2:
                        dve.wait_ge(S("down_done"), g - 1)
                    v.tensor_tensor(f_act[:, par, :], f_sg, f_t[0].rearrange("p a b -> p (a b)"), ALU.mult)\
                        .then_inc(S("act_ready"), 1)

                def ada_turn(g, half):
                    return 2 + 16 * f + 2 * (g - g0 - 2) + half + 1

                then(v.memset(f_u[:, :, :, 0:2], 0.0))
                then(v.memset(f_acc, 0.0))
                if f == 0:
                    dve.wait_ge(S("cact_done"), 1)
                for i in (0, 1):
                    step(g0 + i, i, (g0 + i) % 2)
                start = done[1]
                with dve.Fori(0, 4) as j:
                    per = 2 * 7
                    done[0] = per * j
                    for s in range(2):
                        i = 2 * j + s + 2
                        step(g0 + i, i, (g0 + s) % 2, ada=16 * (2 * j + s + 1))
                    assert done[1] - start == per
                done[0], done[1] = 0, start + 4 * per
                i = FF_STEPS - 1
                step(g0 + i, i, (g0 + i) % 2)
                modulation(f, 0, 4)
                for m in range(4):
                    if m < 3:
                        dve.wait_ge(S("out_bank"), 3 * f + m + 1)
                    else:
                        dve.wait_ge(S("down_done"), g0 + FF_STEPS)
                    add_pair(m, pb[m])
                    if f == 0:
                        gained(2, xg, "kv_norm", "xg_ready", pairs=[m])
                modulation(f, 4, 6)

            ffn(0, 1, 2)

            gained(2, a_xq, "b_norm", "xq_ready")
            residual_norm(2)
            mean_square(2, pb[7][:, 0:T], ms[:, 0:T], D)
            newton(3, ms[:, 0:T], rbc, nwt[:, 0:T])
            dve.wait_ge(S("rcol_turned"), 2)
            v.tensor_copy(rcol[:, 0:1], pb[7][:, 0:1])
            v.tensor_copy(rcol[:, 1:2], pb[7][:, P:P + 1]).then_inc(S("rcol_done"), 1)
            dve.wait_ge(S("gbc_in"), 32)
            for i, x in ((0, a_kt), (1, a_qt)):
                nn = 4 + i
                dve.wait_ge(S("hsq_done"), i + 1)
                y16 = sml[:, 32:48]
                then(v.tensor_reduce(sml[:, 0:16], a_sq.rearrange("p (h d) -> p h d", d=A_DH), AX.X, ALU.add))
                v.tensor_scalar(sml[:, 0:16], sml[:, 0:16], 1.0 / A_DH, EPS, ALU.mult, ALU.add)\
                    .then_inc(S("ms_done"), 1)
                dve.wait_ge(S("ms_done"), 2 + i)
                dve.wait_ge(S("guess_done"), nn + 1)
                then(v.tensor_scalar(sml[:, 0:16], sml[:, 0:16], -0.5, None, ALU.mult))
                newton(nn, sml[:, 0:16], y16, sml[:, 48:64])
                xh = x.rearrange("p b (h d) -> p (b h) d", d=A_DH)
                then(v.tensor_tensor(xh, xh, y16.unsqueeze(2).broadcast_to([P, 16, A_DH]), ALU.mult))
                gain = sml[:, 64 + 32 * i:96 + 32 * i].unsqueeze(1).broadcast_to([P, 16, ROT])
                then(v.tensor_tensor(xh[:, :, 0:ROT], xh[:, :, 0:ROT], gain, ALU.mult))
                x4 = x.rearrange("p b (h d) -> p b h d", d=A_DH)
                cos, sin = [pc(name, TB * HALF).rearrange("p (b d) -> p b d", b=TB) for name in ("cos", "sin")]
                for b in range(TB):
                    x1, x2 = x4[:, b, :, 0:HALF], x4[:, b, :, HALF:ROT]
                    cb = cos[:, b, :].unsqueeze(1).broadcast_to([P, 8, HALF])
                    sb_ = sin[:, b, :].unsqueeze(1).broadcast_to([P, 8, HALF])
                    for r, (u, w) in enumerate(((x1, cb), (x2, sb_), (x2, cb), (x1, sb_))):
                        n = link(v.tensor_tensor(a_rot[r][:, b, :, :], u, w, ALU.mult))
                    after(n)
                    v.tensor_tensor(x1, a_rot[0][:, b, :, :], a_rot[1][:, b, :, :], ALU.subtract)
                    n = v.tensor_tensor(x2, a_rot[2][:, b, :, :], a_rot[3][:, b, :, :], ALU.add)
                    if b == TB - 1:
                        n.then_inc(S("rot_done"), 1)

            def attention(a, scale, added, between=None):
                for n in range(9):
                    if n < 8:
                        h = 8 * a + n
                        dve.wait_ge(S("scores_done"), h + 1)
                        if n >= 2:
                            dve.wait_ge(S("exp_done"), 2 * (h - 1))
                        x, extra, at = sc_sb[n % 2], added(n), 136 + 2 * (n % 2)
                        for b, (lo, hi) in enumerate(((0, P), (P, DIAG))):
                            ins = v.tensor_tensor_reduce(x[:, lo:hi], pb[n % 2][:, lo:hi], extra[:, lo:hi],
                                                         -scale, 3.4e38, ALU.add, ALU.min,
                                                         sml[:, at + b:at + b + 1])
                        ins.then_inc(S("max_done"), 1)
                    if n >= 1:
                        h = 8 * a + n - 1
                        dve.wait_ge(S("exp_done"), 2 * (h + 1))
                        p, at = p_sb[(n - 1) % 2], 140 + 2 * ((n - 1) % 2)
                        then(v.reciprocal(sml[:, at + 4:at + 6], sml[:, at:at + 2]))
                        v.tensor_scalar(p[:, 0:P], p[:, 0:P], sml[:, at + 4:at + 5], None, ALU.mult)
                        v.tensor_scalar(p[:, P:DIAG], p[:, P:DIAG], sml[:, at + 5:at + 6], None, ALU.mult)\
                            .then_inc(S("p_ready"), 1)
                    if between is not None:
                        between(n)

            attention(0, A_DH ** -0.5, lambda n: pc("mask_ts", DIAG))
            for m in range(4):
                product(dve, 28 + m)
                add_pair(m, pb[m])
                gained(3, xg, "f_norm", "xg_ready", at=DC, pairs=[m])
            ffn(1, 3, 6)

            def layer(l):
                n, nn, ns = 32 + 16 * l, 7 + 4 * l, 4 + 4 * l
                gp, gq = sml[:, 148:156], sml[:, 172:180]
                a = COLS["g_pre_2"][0] + 8 * l
                then(v.scalar_tensor_tensor(gp, mod[:, l, 8:16], 1.0, cols[:, a:a + 8], ALU.add, ALU.mult))
                a = COLS["g_post_2"][0] + 8 * l
                then(v.tensor_tensor(gq, mod[:, l, 16:24], cols[:, a:a + 8], ALU.mult))
                residual_norm(4 + l)
                mean_square(ns, pb[7][:, 0:T], ms[:, 0:T], D)
                newton(nn, ms[:, 0:T], rbc, nwt[:, 0:T])
                dve.wait_ge(S("h_ready"), 20 + 4 * l)
                for k in range(DC):
                    v.scalar_tensor_tensor(xg[:, k, :], hT[:, k, :], gp[:, k:k + 1], rbc, ALU.mult, ALU.mult)\
                        .then_inc(S("xn_done"), 1)
                v.memset(b_a[:, :, 0:TAPS - 1], 0.0)
                dve.wait_ge(S("cq_out"), 6 * l + 5)
                v.tensor_tensor(sq[:, 1, :], sq[:, 1, :], sq[:, 0, :], ALU.add).then_inc(S("sum_done"), 1)
                mean_square(ns + 1, pb[3][:, 0:T], ms[:, 0:T], 256)
                mean_square(ns + 1, pb[3][:, T:2 * T], ms[:, T:2 * T], 128)
                newton(nn + 1, ms[:, :], rstd[:, :], nwt[:, :])
                for c in range(2):
                    v.scalar_tensor_tensor(b_cqn[:, c, :], b_cq[:, c, :], col("q_norm_g_2", 2 * l + c), rbc,
                                           ALU.mult, ALU.mult)
                v.scalar_tensor_tensor(b_kvn, b_kv, col("kv_norm_g_2", l), rstd[:, T:2 * T],
                                       ALU.mult, ALU.mult).then_inc(S("cqn_done"), 1)
                dve.wait_ge(S("wcol_turned"), l + 1)
                v.tensor_scalar(wcol, pb[2][:, 0:16].rearrange("p (a b) -> p a b", a=TB),
                                IDX_HEADS ** -0.5 * D_IDX ** -0.5, None, ALU.mult).then_inc(S("wcol_done"), 1)

                def glu(i):
                    dve.wait_ge(S("glu_gate"), 2 * l + i + 1)
                    product(dve, n + (2, 5)[i])
                    v.tensor_tensor(b_a[:, 2 * i:2 * i + 2, TAPS - 1:TAPS - 1 + T], three(pb[0][:, :], 2), b_sg,
                                    ALU.mult).then_inc(S("glu_done"), 1)

                glu(0)
                marks = [None] * CC

                def taps(i, first, end):
                    for tap in range(first, end):
                        for c in (2 * i, 2 * i + 1):
                            if tap == 1:
                                dve.wait_ge(S("conv0_done"), CC * l + c + 1)
                            else:
                                after(marks[c])
                            marks[c] = link(v.scalar_tensor_tensor(
                                b_y[:, c, :], b_a[:, c, tap:tap + T], col("conv_w_2", 124 * l + 4 * tap + c),
                                b_y[:, c, :], ALU.mult, ALU.add))

                TAPS_FIRST = 15
                BESIDE = (3, 5, 5, 5, 5, 5, 5, 3, 5)
                taps(0, 1, 1 + TAPS_FIRST)
                dve.wait_ge(S("wcol_done"), l + 1)
                for r, heads in enumerate(IDX_ORDER):
                    b = 1 if r < 4 else 0
                    wide = P * (b + 1)
                    acc = ts[:, P:DIAG] if b else ts[:, 0:P]
                    dve.wait_ge(S("relu_done"), 6 * l + r + 1)
                    for i, h in enumerate(heads):
                        prev = acc
                        if i > 0:
                            after(last)
                        elif r in (0, 4):
                            prev = pc("mask_top", DIAG)[:, P:DIAG] if b else pc("mask_top", P)
                        else:
                            dve.wait_ge(S("relu_read"), 6 * l + r)
                        ins = v.scalar_tensor_tensor(acc, relu[r % 2][:, wide * i:wide * (i + 1)],
                                                     wcol[:, b, h:h + 1], prev, ALU.mult, ALU.add)
                        if i < len(heads) - 1:
                            last = link(ins)
                        else:
                            ins.then_inc(S("relu_read"), 1)
                dve.wait_ge(S("relu_read"), 6 * l + 6)
                for _ in range(TOPK // 8):
                    m = [link(v.max(best[:, b, :], ts[:, P * b:DIAG if b else P])) for b in range(TB)]
                    for b in range(TB):
                        after(m[b])
                        x = ts[:, P:DIAG] if b else ts[:, 0:P]
                        m[b] = link(v.match_replace(x, best[:, b, :], x, PICKED))
                    after(m[1])
                then(v.tensor_scalar(kmask, ts, -3.2e38, NEG, ALU.is_gt, ALU.mult))
                v.tensor_tensor(kmask, kmask, pc("mask_ts", DIAG), ALU.add).then_inc(S("kmask_done"), 1)

                glu(1)

                def masked(h):
                    dve.wait_ge(S("am_done"), 8 * l + h + 1)
                    return am[h % 2]

                def taps_beside(n_head):
                    left = TAPS - 1 - TAPS_FIRST
                    lo = sum(BESIDE[:n_head])
                    hi = lo + BESIDE[n_head]
                    if lo < left:
                        taps(0, 1 + TAPS_FIRST + lo, 1 + TAPS_FIRST + min(hi, left))
                    if hi > left:
                        taps(1, 1 + max(lo - left, 0), min(1 + hi - left, TAPS))

                attention(1 + l, KV_LORA ** -0.5, masked,
                          lambda n_head: taps_beside(n_head) if n_head < 8 else None)
                def gate_attention(m):
                    dve.wait_ge(S("gates_out"), 2 * l + 1)
                    dve.wait_ge(S("uv_done"), 2 * l + m + 1)
                    x = y2[:, 4 + 2 * m:6 + 2 * m, :]
                    v.tensor_tensor(x, x, three(pb[m][:, :], 2), ALU.mult).then_inc(S("y2_attn"), 1)

                taps_beside(8)
                gate_attention(0)
                gate_attention(1)
                taps(1, 1 + sum(BESIDE) - (TAPS - 1 - TAPS_FIRST), TAPS)
                after(marks[3])
                then(v.tensor_tensor(sq[:, 0:2, :], b_y[:, 0:2, :], b_y[:, 2:4, :], ALU.add))
                v.tensor_tensor(sq[:, 0, :], sq[:, 0, :], sq[:, 1, :], ALU.add).then_inc(S("sum_done"), 1)
                dve.wait_ge(S("ss_done"), ns + 3)
                mean = pb[2][:, 0:T].unsqueeze(1).broadcast_to([P, CC, T])
                v.scalar_tensor_tensor(b_yn, mean, -1.0 / D_CONV, b_y, ALU.mult, ALU.add)\
                    .then_inc(S("yn_done"), 1)
                dve.wait_ge(S("ynsq_done"), l + 1)
                fold(sq, 4, "sum_done")
                mean_square(ns + 3, pb[3][:, 0:T], ms[:, 0:T], D_CONV)
                newton(nn + 2, ms[:, 0:T], rbc, nwt[:, 0:T])
                for c in range(CC):
                    v.scalar_tensor_tensor(b_z[:, c, :], b_yn[:, c, :], col("conv_ln_g_2", 4 * l + c), rbc,
                                           ALU.mult, ALU.mult).then_inc(S("z_done"), 1)
                dve.wait_ge(S("gates_out"), 2 * l + 2)
                for m in range(2):
                    if m == 0:
                        dve.wait_ge(S("pw2_first"), l + 1)
                    else:
                        product(dve, n + 11)
                    x = y2[:, 2 * m:2 * m + 2, :]
                    v.tensor_tensor(x, x, three(pb[m][:, :], 2), ALU.mult).then_inc(S("y2_conv"), 1)
                dve.wait_ge(S("out_sq"), 4 * l + 4)
                a, y = sml[:, 4:6], sml[:, 8:10]
                then(v.tensor_tensor(a, sml[:, 0:2], sml[:, 2:4], ALU.add))
                v.tensor_scalar(a, a, 1.0 / D, EPS, ALU.mult, ALU.add).then_inc(S("ms_done"), 1)
                dve.wait_ge(S("ms_done"), 4 + l)
                dve.wait_ge(S("guess_done"), nn + 4)
                then(v.tensor_scalar(a, a, -0.5, None, ALU.mult))
                newton(nn + 3, a, y, sml[:, 10:12])
                for b in range(TB):
                    v.tensor_scalar(diag[:, b, :], ident, y[:, b:b + 1], None, ALU.mult)\
                        .then_inc(S("diag_done"), 1)
                for m in range(4):
                    dve.wait_ge(S("y_turned"), 4 * l + m + 1)
                    for c in range(2):
                        x = hT[:, 2 * m + c, :]
                        ins = v.scalar_tensor_tensor(x, pb[m][:, T * c:T * (c + 1)],
                                                     gq[:, 2 * m + c:2 * m + c + 1], x, ALU.mult, ALU.add)
                    ins.then_inc(S("h_ready"), 1)

            for l in range(DEPTH):
                layer(l)


INPUTS = ["x", "a_norm", "a_w_in", "a_b_gates", "a_h_norm", "a_w_out", "kv_norm", "w_kv", "k_norm", "b_norm",
          "b_w_q", "b_q_norm", "b_w_o", "f_norm", "f_w_up", "f_conv_w", "f_conv_b", "f_w_down", "c_2",
          "w_ada_2", "b_ada_2", "g_pre_2", "w_in_2", "conv_w_2", "conv_b_2", "conv_ln_g_2", "conv_ln_b_2",
          "w_pw2_2", "q_norm_g_2", "w_uq_2", "w_qidx_2", "kv_norm_g_2", "w_uv_2", "rel_bias_2", "w_out_2",
          "g_post_2"]


def kernel(**inputs):
    import concourse.bacc as bacc
    from concourse.bass_utils import run_bass_kernel_spmd

    nc = bacc.Bacc("TRN2", target_bir_lowering=False, num_devices=1)
    arrays, handles = {}, {}
    for name in INPUTS:
        a = np.ascontiguousarray(inputs[name])
        arrays[f"in_{name}"] = a
        handles[name] = nc.dram_tensor(f"in_{name}", a.shape, mybir.dt.from_np(a.dtype), kind="ExternalInput").ap()
    a = shape_constants()
    arrays["in_consts"] = a
    handles["consts"] = nc.dram_tensor("in_consts", a.shape, F32, kind="ExternalInput").ap()
    out = nc.dram_tensor("out", (1, T, D), F32, kind="ExternalOutput").ap()
    model(nc, handles, out)
    return run_bass_kernel_spmd(nc, [arrays], core_ids=[0]).results[0]["out"]
```
